# Optimizing a Trainium2 kernel written in Bass

```python
import jax, jax.numpy as jnp
from jax import lax
import numpy as np

D_MODEL = 1024
BATCH = 1
SEQ = 256
DEPTH = 2

HEAD_DIM = 64
N_HEADS_A = 16
N_HEADS_B = 16
N_KV_GROUPS_B = 4
HEADS_PER_GROUP = N_HEADS_B // N_KV_GROUPS_B
Q_BLOCK = 128
ROPE_THETA = 500000.0
ROPE_DIM = HEAD_DIM // 4
CMP_BLOCK = 64
SEL_BLOCK = CMP_BLOCK
N_SELECT = 16
WINDOW = 512
SEL_Q_CHUNK = 64
CMP_HIDDEN = 256
N_EXPERTS = 64
TOP_K = 8
D_EXPERT = 256
D_SHARED = 256
ROUTED_SCALE = 2.5
MOE_BLOCK = 256
N_A_LAYERS = DEPTH // 2
N_B_LAYERS = DEPTH - N_A_LAYERS
EPS = 1e-6
FORCE_SCORE = 1e4

kernel_name = 'fox_nsa_yoco_moe_adaln_trunk'

def rmsnorm(x, gain):
    xf = x.astype(jnp.float32)
    xf = xf * lax.rsqrt(jnp.mean(xf * xf, axis=-1, keepdims=True) + EPS)
    return (xf * gain.astype(jnp.float32)).astype(x.dtype)

def modulate(xn, shift, scale):
    return xn * (1 + scale[:, None, :]) + shift[:, None, :]

def rope_tables(positions, dtype):
    inv_freq = ROPE_THETA ** (-jnp.arange(0, ROPE_DIM, 2, dtype=jnp.float32) / ROPE_DIM)
    ang = positions.astype(jnp.float32)[..., None] * inv_freq
    return jnp.cos(ang)[:, :, None, :].astype(dtype), jnp.sin(ang)[:, :, None, :].astype(dtype)

def apply_rope(x, cos, sin):
    half = ROPE_DIM // 2
    x1 = x[..., :half]
    x2 = x[..., half:ROPE_DIM]
    return jnp.concatenate([x1 * cos - x2 * sin, x2 * cos + x1 * sin, x[..., ROPE_DIM:]], axis=-1)

def forgetting_attention(u, w_in, b_f, q_gain, k_gain, w_o):
    B, S, _ = u.shape
    hd = N_HEADS_A * HEAD_DIM
    proj = u @ w_in
    q = rmsnorm(proj[..., :hd].reshape(B, S, N_HEADS_A, HEAD_DIM), q_gain)
    k = rmsnorm(proj[..., hd:2 * hd].reshape(B, S, N_HEADS_A, HEAD_DIM), k_gain)
    v = proj[..., 2 * hd:3 * hd].reshape(B, S, N_HEADS_A, HEAD_DIM)
    log_f = jax.nn.log_sigmoid((proj[..., 3 * hd:] + b_f).astype(jnp.float32))
    cum = jnp.cumsum(log_f, axis=1)
    cum_k = cum.transpose(0, 2, 1)
    nqb = S // Q_BLOCK
    q_blocks = q.reshape(B, nqb, Q_BLOCK, N_HEADS_A, HEAD_DIM).transpose(1, 0, 2, 3, 4)
    cum_blocks = cum.reshape(B, nqb, Q_BLOCK, N_HEADS_A).transpose(1, 0, 2, 3)
    key_pos = jnp.arange(S)
    scale = HEAD_DIM ** -0.5

    def block(args):
        qb, cq, bi = args
        logits = jnp.einsum('bqhd,bkhd->bhqk', qb, k, preferred_element_type=jnp.float32) * scale
        logits = logits + (cq.transpose(0, 2, 1)[..., None] - cum_k[:, :, None, :])
        q_pos = bi * Q_BLOCK + jnp.arange(Q_BLOCK)
        mask = key_pos[None, :] <= q_pos[:, None]
        p = jax.nn.softmax(jnp.where(mask[None, None], logits, -jnp.inf), axis=-1)
        return jnp.einsum('bhqk,bkhd->bqhd', p.astype(v.dtype), v)

    o = lax.map(block, (q_blocks, cum_blocks, jnp.arange(nqb)))
    o = o.transpose(1, 0, 2, 3, 4).reshape(B, S, hd)
    return o @ w_o

def shared_kv(h, cond, norm_kv, w_ada_kv, b_ada_kv, w_kv, pe_k, pe_v, w_ck1, w_ck2, w_cv1, w_cv2,
              k_gains, cos, sin):
    B, S, _ = h.shape
    shift, scale = jnp.split(cond @ w_ada_kv + b_ada_kv, 2, axis=-1)
    s = modulate(rmsnorm(h, norm_kv), shift, scale)
    kv = (s @ w_kv).reshape(B, S, 6, N_KV_GROUPS_B, HEAD_DIM)
    nb = S // CMP_BLOCK

    def compress(t, pe, w1, w2):
        blocks = t.reshape(B, nb, CMP_BLOCK, N_KV_GROUPS_B, HEAD_DIM) + pe[None, None, :, None, :]
        flat = blocks.transpose(0, 1, 3, 2, 4).reshape(B, nb, N_KV_GROUPS_B, CMP_BLOCK * HEAD_DIM)
        return jax.nn.silu(flat @ w1) @ w2

    k_cmp = rmsnorm(compress(kv[:, :, 0], pe_k, w_ck1, w_ck2), k_gains[0])
    v_cmp = compress(kv[:, :, 1], pe_v, w_cv1, w_cv2)
    k_sel = apply_rope(rmsnorm(kv[:, :, 2], k_gains[1]), cos, sin)
    v_sel = kv[:, :, 3]
    k_win = apply_rope(rmsnorm(kv[:, :, 4], k_gains[2]), cos, sin)
    v_win = kv[:, :, 5]
    return (k_cmp, v_cmp, k_sel, v_sel, k_win, v_win)

def selected_branch(q_rot, k_sel, v_sel, sel_idx):
    B, S, G, HPG, Dh = q_rot.shape
    nb = S // SEL_BLOCK
    nc = S // SEL_Q_CHUNK
    n_sel = sel_idx.shape[-1]
    k_blk = k_sel.reshape(B, nb, SEL_BLOCK, G, Dh).transpose(0, 3, 1, 2, 4)
    v_blk = v_sel.reshape(B, nb, SEL_BLOCK, G, Dh).transpose(0, 3, 1, 2, 4)
    qc = q_rot.reshape(B, nc, SEL_Q_CHUNK, G, HPG, Dh).transpose(1, 0, 2, 3, 4, 5)
    ic = sel_idx.reshape(B, nc, SEL_Q_CHUNK, G, n_sel).transpose(1, 0, 2, 3, 4)
    b_ix = jnp.arange(B)[:, None, None, None]
    g_ix = jnp.arange(G)[None, None, :, None]
    scale = Dh ** -0.5

    def chunk(args):
        qb, idx, ci = args
        kg = k_blk[b_ix, g_ix, idx]
        vg = v_blk[b_ix, g_ix, idx]
        logits = jnp.einsum('bqghd,bqgnkd->bqghnk', qb, kg, preferred_element_type=jnp.float32) * scale
        key_pos = idx[..., None] * SEL_BLOCK + jnp.arange(SEL_BLOCK)
        q_pos = ci * SEL_Q_CHUNK + jnp.arange(SEL_Q_CHUNK)
        mask = key_pos <= q_pos[None, :, None, None, None]
        logits = jnp.where(mask[:, :, :, None], logits, -jnp.inf)
        p = jax.nn.softmax(logits.reshape(B, SEL_Q_CHUNK, G, HPG, n_sel * SEL_BLOCK), axis=-1)
        return jnp.einsum('bqghm,bqgmd->bqghd', p.astype(vg.dtype),
                          vg.reshape(B, SEL_Q_CHUNK, G, n_sel * SEL_BLOCK, Dh))

    o = lax.map(chunk, (qc, ic, jnp.arange(nc)))
    return o.transpose(1, 0, 2, 3, 4, 5).reshape(B, S, G * HPG, Dh)

def window_branch(q_rot, k_win, v_win):
    B, S, G, HPG, Dh = q_rot.shape
    nq = S // Q_BLOCK
    span = WINDOW + Q_BLOCK
    kp = jnp.pad(k_win, ((0, 0), (WINDOW, 0), (0, 0), (0, 0)))
    vp = jnp.pad(v_win, ((0, 0), (WINDOW, 0), (0, 0), (0, 0)))
    qb_all = q_rot.reshape(B, nq, Q_BLOCK, G, HPG, Dh).transpose(1, 0, 2, 3, 4, 5)
    scale = Dh ** -0.5

    def block(args):
        qb, bi = args
        start = bi * Q_BLOCK
        kb = lax.dynamic_slice_in_dim(kp, start, span, axis=1)
        vb = lax.dynamic_slice_in_dim(vp, start, span, axis=1)
        logits = jnp.einsum('bqghd,bkgd->bqghk', qb, kb, preferred_element_type=jnp.float32) * scale
        q_pos = start + jnp.arange(Q_BLOCK)
        k_pos = start - WINDOW + jnp.arange(span)
        diff = q_pos[:, None] - k_pos[None, :]
        mask = (diff >= 0) & (diff < WINDOW) & (k_pos >= 0)[None, :]
        p = jax.nn.softmax(jnp.where(mask[None, :, None, None, :], logits, -jnp.inf), axis=-1)
        return jnp.einsum('bqghk,bkgd->bqghd', p.astype(vb.dtype), vb)

    o = lax.map(block, (qb_all, jnp.arange(nq)))
    return o.transpose(1, 0, 2, 3, 4, 5).reshape(B, S, G * HPG, Dh)

def nsa_attention(u, kv, cos, sin, w_in, b_gate, q_gain, w_o):
    k_cmp, v_cmp, k_sel, v_sel, k_win, v_win = kv
    B, S, _ = u.shape
    hd = N_HEADS_B * HEAD_DIM
    proj = u @ w_in
    q = rmsnorm(proj[..., :hd].reshape(B, S, N_HEADS_B, HEAD_DIM), q_gain)
    gates = jax.nn.sigmoid(proj[..., hd:] + b_gate).reshape(B, S, N_HEADS_B, 3)
    q_rot = apply_rope(q, cos, sin).reshape(B, S, N_KV_GROUPS_B, HEADS_PER_GROUP, HEAD_DIM)
    q_plain = q.reshape(B, S, N_KV_GROUPS_B, HEADS_PER_GROUP, HEAD_DIM)
    t_pos = jnp.arange(S)
    nb = S // CMP_BLOCK
    blk = jnp.arange(nb)
    logits = jnp.einsum('bsghd,bngd->bsghn', q_plain, k_cmp, preferred_element_type=jnp.float32) * HEAD_DIM ** -0.5
    vis = ((blk[None, :] + 1) * CMP_BLOCK - 1 <= t_pos[:, None])[None, :, None, None, :]
    p_cmp = jnp.where(vis, jax.nn.softmax(jnp.where(vis, logits, -1e30), axis=-1), 0.0)
    o_cmp = jnp.einsum('bsghn,bngd->bsghd', p_cmp.astype(v_cmp.dtype), v_cmp).reshape(B, S, N_HEADS_B, HEAD_DIM)
    importance = p_cmp.sum(axis=3)
    cur = t_pos // SEL_BLOCK
    forced = (blk[None, :] == 0) | (blk[None, :] == cur[:, None]) | (blk[None, :] == cur[:, None] - 1)
    future = blk[None, :] > cur[:, None]
    importance = jnp.where(forced[None, :, None, :], FORCE_SCORE,
                           jnp.where(future[None, :, None, :], -FORCE_SCORE, importance))
    n_sel = min(N_SELECT, nb)
    _, sel_idx = lax.top_k(importance, n_sel)
    o_sel = selected_branch(q_rot, k_sel, v_sel, sel_idx)
    o_win = window_branch(q_rot, k_win, v_win)
    o = gates[..., 0:1] * o_cmp + gates[..., 1:2] * o_sel + gates[..., 2:3] * o_win
    return o.reshape(B, S, hd) @ w_o

def moe_ffn(u, w_router, b_router, w_eg, w_eu, w_ed, w_sg, w_su, w_sd):
    B, S, D = u.shape
    T = B * S
    h = u.reshape(T, D)
    scores = jax.nn.sigmoid(jnp.matmul(h, w_router, preferred_element_type=jnp.float32))
    _, top_e = lax.top_k(scores + b_router.astype(jnp.float32), TOP_K)
    top_s = jnp.take_along_axis(scores, top_e, axis=-1)
    top_w = top_s / jnp.sum(top_s, axis=-1, keepdims=True) * ROUTED_SCALE
    n_assign = T * TOP_K
    flat_e = top_e.reshape(-1)
    flat_t = jnp.repeat(jnp.arange(T, dtype=jnp.int32), TOP_K)
    flat_w = top_w.reshape(-1)
    order = jnp.argsort(flat_e)
    se, st, sw = flat_e[order], flat_t[order], flat_w[order]
    counts = jnp.bincount(flat_e, length=N_EXPERTS)
    padded = (counts + MOE_BLOCK - 1) // MOE_BLOCK * MOE_BLOCK
    pad_end = jnp.cumsum(padded)
    pad_start = pad_end - padded
    grp_start = jnp.cumsum(counts) - counts
    dest = pad_start[se] + (jnp.arange(n_assign) - grp_start[se])
    n_blocks = (n_assign + MOE_BLOCK - 1) // MOE_BLOCK + N_EXPERTS
    n_rows = n_blocks * MOE_BLOCK
    row_tok = jnp.zeros((n_rows,), jnp.int32).at[dest].set(st)
    row_w = jnp.zeros((n_rows,), h.dtype).at[dest].set(sw.astype(h.dtype))
    block_e = jnp.minimum(jnp.searchsorted(pad_end, jnp.arange(n_blocks) * MOE_BLOCK, side='right'),
                          N_EXPERTS - 1)

    def expert_block(args):
        tok, e = args
        xb = h[tok]
        return (jax.nn.silu(xb @ w_eg[e]) * (xb @ w_eu[e])) @ w_ed[e]

    y_rows = lax.map(expert_block, (row_tok.reshape(n_blocks, MOE_BLOCK), block_e))
    routed = jax.ops.segment_sum(y_rows.reshape(n_rows, D) * row_w[:, None], row_tok, num_segments=T)
    shared = (jax.nn.silu(h @ w_sg) * (h @ w_su)) @ w_sd
    return (routed + shared).reshape(B, S, D)

def setup_inputs(seed: int = 0) -> dict:
    key = jax.random.key(seed)
    ks = jax.random.split(key, 36)
    D = D_MODEL
    HDA = N_HEADS_A * HEAD_DIM
    HDB = N_HEADS_B * HEAD_DIM
    G = N_KV_GROUPS_B

    def nrm(k, shape, s):
        return jax.random.normal(k, shape, jnp.float32) * s

    positions = (jax.random.randint(ks[2], (BATCH, 1), 0, 4096, dtype=jnp.int32)
                 + jnp.arange(SEQ, dtype=jnp.int32)[None, :])
    return {
        'x': nrm(ks[0], (BATCH, SEQ, D), 1.0),
        'c': nrm(ks[1], (BATCH, D), 1.0),
        'positions': positions,
        'w_ada': nrm(ks[3], (DEPTH, D, 6 * D), 0.5 * D ** -0.5),
        'b_ada': nrm(ks[4], (DEPTH, 6 * D), 0.02),
        'norm_mix': 1.0 + nrm(ks[5], (DEPTH, D), 0.05),
        'norm_ffn': 1.0 + nrm(ks[6], (DEPTH, D), 0.05),
        'w_in_a': nrm(ks[7], (N_A_LAYERS, D, 3 * HDA + N_HEADS_A), D ** -0.5),
        'b_f_a': 3.0 + nrm(ks[8], (N_A_LAYERS, N_HEADS_A), 0.1),
        'qnorm_a': 1.0 + nrm(ks[9], (N_A_LAYERS, HEAD_DIM), 0.05),
        'knorm_a': 1.0 + nrm(ks[10], (N_A_LAYERS, HEAD_DIM), 0.05),
        'w_o_a': nrm(ks[11], (N_A_LAYERS, HDA, D), HDA ** -0.5),
        'norm_kv': 1.0 + nrm(ks[12], (D,), 0.05),
        'w_ada_kv': nrm(ks[13], (D, 2 * D), 0.5 * D ** -0.5),
        'b_ada_kv': nrm(ks[14], (2 * D,), 0.02),
        'w_kv_b': nrm(ks[15], (D, 6 * G * HEAD_DIM), D ** -0.5),
        'pe_cmp_k': nrm(ks[16], (CMP_BLOCK, HEAD_DIM), 0.1),
        'pe_cmp_v': nrm(ks[17], (CMP_BLOCK, HEAD_DIM), 0.1),
        'w_cmp_k1': nrm(ks[18], (CMP_BLOCK * HEAD_DIM, CMP_HIDDEN), (CMP_BLOCK * HEAD_DIM) ** -0.5),
        'w_cmp_k2': nrm(ks[19], (CMP_HIDDEN, HEAD_DIM), CMP_HIDDEN ** -0.5),
        'w_cmp_v1': nrm(ks[20], (CMP_BLOCK * HEAD_DIM, CMP_HIDDEN), (CMP_BLOCK * HEAD_DIM) ** -0.5),
        'w_cmp_v2': nrm(ks[21], (CMP_HIDDEN, HEAD_DIM), CMP_HIDDEN ** -0.5),
        'knorm_b': 1.0 + nrm(ks[22], (3, HEAD_DIM), 0.05),
        'w_in_b': nrm(ks[23], (N_B_LAYERS, D, HDB + 3 * N_HEADS_B), D ** -0.5),
        'b_gate_b': nrm(ks[24], (N_B_LAYERS, 3 * N_HEADS_B), 0.1),
        'qnorm_b': 1.0 + nrm(ks[25], (N_B_LAYERS, HEAD_DIM), 0.05),
        'w_o_b': nrm(ks[26], (N_B_LAYERS, HDB, D), HDB ** -0.5),
        'w_router': nrm(ks[27], (DEPTH, D, N_EXPERTS), D ** -0.5),
        'b_router': nrm(ks[28], (DEPTH, N_EXPERTS), 0.01),
        'w_exp_gate': nrm(ks[29], (DEPTH, N_EXPERTS, D, D_EXPERT), D ** -0.5),
        'w_exp_up': nrm(ks[30], (DEPTH, N_EXPERTS, D, D_EXPERT), D ** -0.5),
        'w_exp_down': nrm(ks[31], (DEPTH, N_EXPERTS, D_EXPERT, D), D_EXPERT ** -0.5),
        'w_sh_gate': nrm(ks[32], (DEPTH, D, D_SHARED), D ** -0.5),
        'w_sh_up': nrm(ks[33], (DEPTH, D, D_SHARED), D ** -0.5),
        'w_sh_down': nrm(ks[34], (DEPTH, D_SHARED, D), D_SHARED ** -0.5),
    }

def reference(x, c, positions, w_ada, b_ada, norm_mix, norm_ffn, w_in_a, b_f_a, qnorm_a, knorm_a,
              w_o_a, norm_kv, w_ada_kv, b_ada_kv, w_kv_b, pe_cmp_k, pe_cmp_v, w_cmp_k1, w_cmp_k2,
              w_cmp_v1, w_cmp_v2, knorm_b, w_in_b, b_gate_b, qnorm_b, w_o_b, w_router, b_router,
              w_exp_gate, w_exp_up, w_exp_down, w_sh_gate, w_sh_up, w_sh_down):
    cos, sin = rope_tables(positions, x.dtype)
    cond = jax.nn.silu(c)
    h = x
    kv = None
    for layer in range(DEPTH):
        ada = cond @ w_ada[layer] + b_ada[layer]
        sh_m, sc_m, g_m, sh_f, sc_f, g_f = jnp.split(ada, 6, axis=-1)
        u = modulate(rmsnorm(h, norm_mix[layer]), sh_m, sc_m)
        if layer < N_A_LAYERS:
            mix = forgetting_attention(u, w_in_a[layer], b_f_a[layer], qnorm_a[layer], knorm_a[layer],
                                       w_o_a[layer])
        else:
            if layer == N_A_LAYERS:
                kv = shared_kv(h, cond, norm_kv, w_ada_kv, b_ada_kv, w_kv_b, pe_cmp_k, pe_cmp_v,
                               w_cmp_k1, w_cmp_k2, w_cmp_v1, w_cmp_v2, knorm_b, cos, sin)
            j = layer - N_A_LAYERS
            mix = nsa_attention(u, kv, cos, sin, w_in_b[j], b_gate_b[j], qnorm_b[j], w_o_b[j])
        h = h + g_m[:, None, :] * mix
        u = modulate(rmsnorm(h, norm_ffn[layer]), sh_f, sc_f)
        h = h + g_f[:, None, :] * moe_ffn(u, w_router[layer], b_router[layer], w_exp_gate[layer],
                                          w_exp_up[layer], w_exp_down[layer], w_sh_gate[layer],
                                          w_sh_up[layer], w_sh_down[layer])
    return h


_drawn_inputs = setup_inputs


def setup_inputs(seed=0):
    import zlib

    import numpy as np

    out = dict(_drawn_inputs(seed))
    spreads = {}
    factors = {'qnorm_a': 3.132,
     'knorm_a': 2.879,
     'norm_kv': 6.124,
     'b_ada_kv': 4.322,
     'pe_cmp_k': 8.0,
     'pe_cmp_v': 8.811,
     'knorm_b': 6.312,
     'b_gate_b': 3.586,
     'qnorm_b': 7.376}
    for name, (base, spread) in spreads.items():
        noise = np.random.default_rng([zlib.crc32(name.encode()), seed]).standard_normal(out[name].shape)
        drawn = base * np.exp(spread * noise) if base else spread * noise
        out[name] = __import__('jax').numpy.asarray(drawn.astype(out[name].dtype))
    for name, factor in factors.items():
        out[name] = (out[name] * factor).astype(out[name].dtype)
    return out
```

```python
from contextlib import ExitStack

import numpy as np

import concourse.bass as bass
from concourse import mybir

F32 = mybir.dt.float32
I32 = mybir.dt.int32
ALU = mybir.AluOpType
ACT = mybir.ActivationFunctionType
AX = mybir.AxisListType

P = 128
D = 1024
SEQ = 256
NT = SEQ // P
KC = D // P
DH = 64
H = 16
G = 4
HPG = H // G
ROPE_HALF = DH // 8
ROPE_THETA = 500000.0
CMP = 64
NB = SEQ // CMP
N_EXP = 64
D_EXP = 256
EPS = 1e-6
MASKED = -1e30
ROUTED_SCALE = 2.5
QK_SCALE = DH ** -0.5

UC = 256
UNIT = KC * UC
SLOTS = 12
BODY = SLOTS // 3
TURNS = N_EXP // BODY
PASS = 64
MAX_PASSES = SEQ // PASS
TABLE = N_EXP + 2

U_ADA = [0, 0]
U_QKV = U_ADA[0] + 6 * D // UC
U_OUT_A = U_QKV + 3 * D // UC
U_SHARED = [U_OUT_A + D // UC, 0]
U_EXPERTS = [U_SHARED[0] + 3, 0]
U_ADA[1] = U_EXPERTS[0] + 3 * N_EXP
U_ADA_KV = U_ADA[1] + 6 * D // UC
U_KV = U_ADA_KV + 2 * D // UC
U_CMP = U_KV + 6 * G * DH // UC
U_Q = U_CMP + 2 * 4
U_OUT_B = U_Q + D // UC
U_SHARED[1] = U_OUT_B + D // UC
U_EXPERTS[1] = U_SHARED[1] + 3
U_END = U_EXPERTS[1] + 3 * N_EXP

SH_M, SC_M, G_M, SH_F, SC_F, G_F = range(6)


class Steps:

    def __init__(self, eng, step):
        self.eng, self.step, self.count = eng, step, {}

    def __call__(self, ins, sem=None):
        sem = sem or self.step
        ins.then_inc(sem, 1)
        self.count[sem.name] = self.count.get(sem.name, 0) + 1
        self.eng.wait_ge(sem, self.count[sem.name])


def attention_batches(kind):
    branches = (0,) if kind == "fox" else (0, 1)
    return [(br, t, g) for br in branches for t in range(NT) for g in range(H // 4)]


def build(nc, a, out):
    with ExitStack() as ctx:
        def sb(name, shape, dt=F32):
            return ctx.enter_context(nc.sbuf_tensor(name, shape, dt))

        sems = {}

        def sem(name):
            if name not in sems:
                sems[name] = ctx.enter_context(nc.semaphore(name))
            return sems[name]

        PS = ctx.enter_context(nc.psum_tensor("PS", [P, 8, 512], F32))
        ring = sb("ring", [P, SLOTS, UNIT])
        h = sb("h", [P, NT, D])
        u = sb("u", [P, NT, D])
        uT = sb("uT", [P, KC, SEQ])
        ada = sb("ada", [P, 6, D])
        gain = sb("gain", [P, D])
        scratch = sb("scratch", [P, 12288])
        ident = sb("ident", [P, P])
        ones = sb("ones", [P, P])
        upto = sb("upto", [P, P])
        before = sb("before", [P, P])
        causal = sb("causal", [P, 2 * P])
        iota = sb("iota", [P, SEQ])
        block_diag = sb("block_diag", [H * NB, H])
        cond = sb("cond", [P, KC])
        pos_i = sb("pos_i", [P, NT], I32)
        freq = sb("freq", [P, ROPE_HALF])
        cos_t = sb("cos_t", [P, NT, ROPE_HALF])
        sin_t = sb("sin_t", [P, NT, ROPE_HALF])
        gain_qa = sb("gain_qa", [P, DH])
        gain_ka = sb("gain_ka", [P, DH])
        gain_qb = sb("gain_qb", [P, DH])
        gain_kb = sb("gain_kb", [P, 3, DH])
        bias_f = sb("bias_f", [P, H])
        bias_gate = sb("bias_gate", [P, 3 * H])
        bias_router = sb("bias_router", [P, 2, N_EXP])
        pe = sb("pe", [P, 2, DH])
        w_gates = sb("w_gates", [P, KC, 3 * H])
        w_forget = w_gates[:, :, 0:H]
        partition_no = sb("partition_no", [P, 1])
        gates = sb("gates", [P, NT, 3 * H])
        small = sb("small", [P, 96])
        stats = sb("stats", [P, 2, 16])
        slot_of = sb("slot_of", [P, NT, TABLE])
        weight_of = sb("weight_of", [P, NT, TABLE])
        passes_i = sb("passes_i", [1, 2, TABLE], I32)

        def cut(at, shape):
            n = int(np.prod(shape))
            v = scratch[:, at:at + n]
            names = " ".join(f"d{i}" for i in range(len(shape)))
            return v if len(shape) == 1 else v.rearrange(f"p ({names}) -> p {names}", **{
                f"d{i}": s for i, s in enumerate(shape)})

        qT = cut(0, [KC, SEQ])
        kz_a = cut(2048, [H, SEQ])
        v_a = cut(6144, [NT, D])
        q_rows = cut(2048, [NT, D])
        kz_b = cut(4096, [2, G, 2, SEQ])
        v_b = cut(8192, [2, NT, G * DH])
        S0 = 9216
        softmax_in = [cut(S0, [4 * SEQ]), cut(S0 + 1024, [4 * SEQ])]
        pT = cut(S0 + 2048, [4 * SEQ])
        squares = cut(S0, [512])
        normed = [cut(S0 + 1024, [512]), cut(S0 + 1536, [512])]
        cond_cols = cut(S0 + 2048, [KC, P])
        ada_kv = cut(0, [2, D])
        doubled = [cut(S0, [NT, G, 2, DH]), cut(S0 + 1024, [NT, G, 2, DH])]
        flat = [cut(2048, [32, G * NB]), cut(2560, [32, G * NB])]
        hidden = cut(3072, [2, G * NB])
        hidden_rep = cut(3104, [2, H * NB])
        kc_rows = cut(3232, [2, DH])
        w_cmp2 = cut(3360, [2, 2, DH])
        kcz = small[:, 0:2 * G * NB].rearrange("p (a b) -> p a b", a=2)
        new_keys = cut(0, [NT, G, DH])
        rope_tmp_k = cut(512, [4 * G * ROPE_HALF])
        v_cmp_rows = cut(640, [DH])
        squares_kv = cut(1024, [512])
        v_diag = cut(S0 + 2048, [H, DH])
        cmp_buf = cut(S0, [NT, H * NB])
        cmp_T = cut(S0 + 256, [SEQ])
        visible = cut(S0 + 512, [NT, NB])
        hidden_mask = cut(S0 + 528, [NT, NB])
        uT_flat = uT[:, :, :].rearrange("p k t -> p (k t)")
        cum = uT_flat[:, 0:2 * P].rearrange("p (t c) -> p t c", t=NT)
        cumT = uT_flat[:, 256:512]
        ncumT = uT_flat[:, 512:768]
        fg = [uT_flat[:, 768 + 32 * i:800 + 32 * i] for i in range(5)]
        head_row = ada[:, 0:2, :].rearrange("p a d -> p (a d)").rearrange("p (h m) -> p h m", h=H)
        x_exp = cut(0, [KC, PASS])
        x_more = cut(512, [KC, PASS])
        one_hot = [cut(1024, [NT, PASS]), cut(1152, [NT, PASS])]
        hot_more = cut(1280, [NT, PASS])
        hot_w = cut(1408, [NT, 2 * PASS])
        hot_wT = cut(1664, [SEQ])
        gate_act = cut(1920, [2, PASS])
        hid = cut(2048, [2, PASS])
        y_rows = cut(2176, [D])
        sh_act = cut(3200, [2, SEQ])
        sh_hid = cut(3712, [2, SEQ])
        scores = cut(4224, [NT, N_EXP])
        chosen_by = cut(4352, [NT, N_EXP])
        replaced = cut(4480, [NT, N_EXP])
        routed = cut(4608, [NT, N_EXP])
        passes_f = cut(4736, [P])
        top8 = cut(4864, [NT, 8])
        rsum = cut(4880, [NT])
        w_router = cut(5120, [KC, N_EXP])
        mod_tmp = cut(8192, [D])
        mod_tmp_q = cut(S0, [D])
        rope_tmp_q = cut(S0 + 1024, [4 * H * ROPE_HALF])
        head_tmp = cut(2048, [4, DH])
        g_tmp = cut(8192, [D])

        slot_loaded = [sem(f"slot_loaded{i}") for i in range(SLOTS)]
        unit_done = sem("unit_done")
        params = sem("params_loaded")
        x_loaded = sem("x_loaded")
        gain_loaded = sem("gain_loaded")
        gain_used = sem("gain_used")
        bias_loaded = sem("ada_bias_loaded")
        bias_kv_loaded = sem("ada_kv_bias_loaded")
        consts = sem("consts_ready")
        pool_step = sem("pool_step")
        dve_step = sem("dve_step")
        act_step = sem("act_step")
        cond_ready = sem("cond_ready")
        layer_added = sem("layer_added")
        router_loaded = sem("router_loaded")
        nsa_params = sem("nsa_params_loaded")
        stored = sem("stored")
        TURNED = ["mix0", "fox_o", "ffn0", "kv", "mix1", "q", "q_rotated", "nsa_o", "ffn1"]
        MODULATED = ["mix0", "ffn0", "kv", "mix1", "ffn1"]
        NORMED = ["mix0", "ffn0", "mix1", "ffn1"]
        HEADS_FROM = {"foxn": 0, "kvn": 8, "qn": 10}
        BATCHES_FROM = {"fox": 0, "nsa": 8}
        rows_turned, rows_copied, rows_modulated = sem("rows_turned"), sem("rows_copied"), sem("rows_modulated")
        row_squares, row_means, row_roots = sem("row_squares"), sem("row_means"), sem("row_roots")
        head_squares, head_means, head_roots = sem("head_squares"), sem("head_means"), sem("head_roots")
        logits_out, scores_read, scores_shifted = sem("logits_out"), sem("scores_read"), sem("scores_shifted")
        probs_ready, probs_turned, probsT_ready = sem("probs_ready"), sem("probs_turned"), sem("probsT_ready")
        heads_out, heads_read = sem("heads_out"), sem("heads_read")
        ada_read = sem("ada_read")
        mix_added = sem("mix_added")

        def landed(eng, n):
            eng.wait_ge(slot_loaded[n % SLOTS], 16 * (n // SLOTS + 1))

        def slot(n, k=KC):
            return ring[:, n % SLOTS, :].rearrange("p (k c) -> p k c", k=k)

        def bcast(ap, shape):
            return ap.to_broadcast(shape)

        MOE_SEMS = ["router_out", "scores_ready", "mask_ready", "ranks_out", "passes_ready", "passes_out",
                    "tables_ready", "shared_act", "shared_hid", "onehot_ready", "gathered", "x_ready",
                    "gu_out", "gate_ready", "hid_ready", "hot_w_ready", "hot_w_turned", "hot_wT_ready",
                    "y_out", "y_ready",
                    "more_onehot", "more_gathered", "more_x", "more_gu", "more_gate", "more_hid",
                    "more_turned", "more_wT", "more_y_out", "more_y", "more_added"]
        moe_sem = [{n: sem(f"{n}{layer}") for n in MOE_SEMS} for layer in range(2)]

        def pe_turn_rows(pe_, src, ready, what, banks_free=()):
            pe_.wait_ge(*ready)
            for s, n in banks_free:
                pe_.wait_ge(s, n)
            for b in range(KC // 2):
                for k in (2 * b, 2 * b + 1):
                    for t in range(NT):
                        mm = pe_.transpose(PS[:, b, (k % 2) * SEQ + t * P:(k % 2) * SEQ + (t + 1) * P],
                                           src[:, t, k * P:(k + 1) * P], ident[:, :])
                mm.then_inc(rows_turned, 1)
            pe_.wait_ge(rows_copied, 4 * TURNED.index(what) + 4)

        def act_copy_turned(done, dst, what):
            for b in range(KC // 2):
                done.eng.wait_ge(rows_turned, 4 * TURNED.index(what) + b + 1)
                done(done.eng.activation(dst[:, 2 * b:2 * b + 2, :].rearrange("p k t -> p (k t)"),
                                         PS[:, b, :], ACT.Copy), rows_copied)

        def pe_rows_unit(pe_, n, bank, lhs):
            landed(pe_, n)
            w = slot(n)
            for t in range(NT):
                for k in range(KC):
                    mm = pe_.matmul(PS[:, bank, t * UC:(t + 1) * UC], lhs[:, k, t * P:(t + 1) * P],
                                    w[:, k, :], start=(k == 0), stop=(k == KC - 1))
            mm.then_inc(unit_done, 1)

        def pe_ada(pe_, u0, n_units, j0):
            for j in range(n_units):
                landed(pe_, u0 + j)
                if j >= 4:
                    pe_.wait_ge(ada_read, j0 + j - 3)
                for k in range(KC):
                    mm = pe_.matmul(PS[:, j % 4, 0:UC], cond_cols[:, k, :], slot(u0 + j)[:, k, :],
                                    start=(k == 0), stop=(k == KC - 1))
                mm.then_inc(unit_done, 1)

        def dve_ada(done, u0, n_units, rows, bias):
            done.eng.wait_ge(*bias)
            for j in range(n_units):
                done.eng.wait_ge(unit_done, u0 + j + 1)
                r = rows[:, j // 4, (j % 4) * UC:(j % 4 + 1) * UC]
                done(done.eng.tensor_tensor(r, PS[:, j % 4, 0:UC], r, ALU.add), ada_read)

        def width(t):
            return (t + 1) * P

        def logit_banks(b):
            return PS[:, 2 * (b % 2):2 * (b % 2) + 2, :].rearrange("p b (i w) -> p (b i) w", i=2)

        def pe_attention(pe_, kind, batches, keys, values):
            b0 = BATCHES_FROM[kind]

            def logits(b):
                br, t, g = batches[b]
                w = width(t)
                if b >= 2:
                    pe_.wait_ge(scores_read, b0 + b - 1)
                o = logit_banks(b)
                for i in range(4):
                    hd = 4 * g + i
                    mm = pe_.matmul(o[:, i, 0:w], qT[:, hd // 2, t * P:(t + 1) * P], keys(br, hd)[:, 0:w],
                                    start=True, stop=(kind != "fox"))
                    if kind == "fox":
                        pe_.matmul(o[:, i, 0:w].rearrange("p (c m) -> p c m", m=P),
                                   cumT[:, t * P:(t + 1) * P],
                                   head_row[:, hd:hd + 1, :].to_broadcast([P, w // P, P]),
                                   start=False, stop=False)
                        mm = pe_.matmul(o[:, i, 0:w], head_row[:, hd, :], ncumT[:, 0:w], start=False, stop=True)
                mm.then_inc(logits_out, 1)

            def turn(b):
                br, t, g = batches[b]
                w = width(t)
                pe_.wait_ge(probs_ready, 4 * (b0 + b + 1))
                p = softmax_in[b % 2]
                for n in range(4 * (t + 1)):
                    mm = pe_.transpose(PS[:, 4 + n // 4, (n % 4) * P:(n % 4 + 1) * P],
                                       p[:, n * P:(n + 1) * P], ident[:, :])
                mm.then_inc(probs_turned, 1)

            def weigh(b):
                br, t, g = batches[b]
                pe_.wait_ge(probsT_ready, b0 + b + 1)
                if b >= 2:
                    pe_.wait_ge(heads_read, b0 + b - 1)
                for i in range(4):
                    for kt in range(t + 1):
                        n = i * (t + 1) + kt
                        mm = pe_.matmul(PS[:, 6 + b % 2, i * DH:(i + 1) * DH], pT[:, n * P:(n + 1) * P],
                                        values(br, kt, 4 * g + i), start=(kt == 0), stop=(kt == t))
                mm.then_inc(heads_out, 1)

            logits(0)
            for b in range(len(batches)):
                if b + 1 < len(batches):
                    logits(b + 1)
                turn(b)
                weigh(b)

        def act_attention(done, kind, batches):
            eng, b0 = done.eng, BATCHES_FROM[kind]
            for b, (br, t, g) in enumerate(batches):
                w = width(t)
                eng.wait_ge(scores_shifted, b0 + b + 1)
                for i in range(4):
                    p = softmax_in[b % 2][:, i * w:(i + 1) * w]
                    done(eng.activation(p, p, ACT.Exp, bias=stats[:, b % 2, 4 + i:5 + i],
                                        accum_out=stats[:, b % 2, 8 + i:9 + i]), probs_ready)
                eng.wait_ge(probs_turned, b0 + b + 1)
                if b >= 1:
                    eng.wait_ge(heads_out, b0 + b)
                n = 4 * w
                done(eng.activation(pT[:, 0:n], PS[:, 4:4 + n // 512, :].rearrange("p b c -> p (b c)"), ACT.Copy),
                     probsT_ready)

        def dve_attention(done, kind, batches, finish):
            eng, b0 = done.eng, BATCHES_FROM[kind]

            def mask(b):
                br, t, g = batches[b]
                w = width(t)
                eng.wait_ge(logits_out, b0 + b + 1)
                if b >= 2:
                    eng.wait_ge(probs_turned, b0 + b - 1)
                s = softmax_in[b % 2][:, 0:4 * w].rearrange("p (i w) -> p i w", i=4)
                done(eng.tensor_tensor(s, logit_banks(b)[:, :, 0:w],
                                       causal[:, 2 * P - w:2 * P].unsqueeze(1).to_broadcast([P, 4, w]), ALU.add),
                     scores_read)
                done(eng.tensor_reduce(stats[:, b % 2, 0:4], s, AX.X, ALU.max))
                done(eng.tensor_scalar(stats[:, b % 2, 4:8], stats[:, b % 2, 0:4], -1.0, None, ALU.mult),
                     scores_shifted)

            def output(b):
                eng.wait_ge(probs_ready, 4 * (b0 + b + 1))
                done(eng.reciprocal(stats[:, b % 2, 12:16], stats[:, b % 2, 8:12]))
                finish(b, PS[:, 6 + b % 2, 0:4 * DH].rearrange("p (i d) -> p i d", i=4), stats[:, b % 2, 12:16])

            for b in range(len(batches)):
                mask(b)
                if b >= 1:
                    output(b - 1)
            output(len(batches) - 1)

        def act_row_norms(done, tag, h_ready):
            done.eng.wait_ge(*h_ready)
            for t in range(NT):
                done(done.eng.activation(u[:, t, :], h[:, t, :], ACT.Square, accum_out=small[:, 64 + t:65 + t]),
                     row_squares)
            i = NORMED.index(tag)
            done.eng.wait_ge(row_means, i + 1)
            done(done.eng.activation(small[:, 68:70], small[:, 66:68], ACT.Sqrt), row_roots)

        def dve_row_norms(done, tag):
            eng = done.eng
            i = NORMED.index(tag)
            eng.wait_ge(row_squares, NT * (i + 1))
            done(eng.tensor_scalar(small[:, 66:68], small[:, 64:66], 1.0 / D, EPS, ALU.mult, ALU.add),
                 row_means)
            eng.wait_ge(row_roots, i + 1)
            done(eng.reciprocal(small[:, 70:72], small[:, 68:70]))

        def dve_modulate(done, shift, scale, n_gain, split, ready, mod_tmp=mod_tmp):
            eng = done.eng
            eng.wait_ge(gain_loaded, 16 * (n_gain + 1))
            done(eng.scalar_tensor_tensor(out=scale, in0=scale, scalar=1.0, in1=gain[:, :],
                                          op0=ALU.add, op1=ALU.mult), gain_used)
            for t in range(NT):
                done(eng.scalar_tensor_tensor(out=mod_tmp, in0=h[:, t, :], scalar=small[:, 70 + t:71 + t],
                                              in1=scale, op0=ALU.mult, op1=ALU.mult))
                if split:
                    o = u[:, t, :].rearrange("p (k q) -> p q k", k=KC)
                    i0 = mod_tmp.rearrange("p (q k) -> p q k", k=KC)
                    i1 = shift.rearrange("p (q k) -> p q k", k=KC)
                else:
                    o, i0, i1 = u[:, t, :], mod_tmp, shift
                done(eng.tensor_tensor(o, i0, i1, ALU.add), ready)

        def dve_add_rows(done, cols, banks, gate_row, ready=None):
            eng = done.eng
            n = cols.stop - cols.start
            tmp = g_tmp[:, 0:2 * n].rearrange("p (t c) -> p t c", t=NT)
            done(eng.tensor_tensor(tmp, banks, gate_row.unsqueeze(1).to_broadcast([P, NT, n]), ALU.mult))
            hc = h[:, :, cols]
            done(eng.tensor_tensor(hc, hc, tmp, ALU.add), ready)

        def act_head_squares(done, tag, i, n, bank, squares=squares):
            i += HEADS_FROM[tag]
            done.eng.wait_ge(unit_done, n + 1)
            if i >= 1:
                done.eng.wait_ge(head_means, i)
            done(done.eng.activation(squares, PS[:, bank, :], ACT.Square), head_squares)
            done.eng.wait_ge(head_means, i + 1)
            done(done.eng.activation(small[:, 80:88], small[:, 72:80], ACT.Sqrt), head_roots)

        def dve_head_norm(done, tag, i, bank, dst, gain_row, ready, squares=squares):
            eng = done.eng
            i += HEADS_FROM[tag]
            eng.wait_ge(head_squares, i + 1)
            done(eng.tensor_reduce(small[:, 72:80], squares.rearrange("p (h d) -> p h d", h=8), AX.X, ALU.add))
            done(eng.tensor_scalar(small[:, 72:80], small[:, 72:80], 1.0 / DH, EPS, ALU.mult, ALU.add),
                 head_means)
            eng.wait_ge(head_roots, i + 1)
            done(eng.reciprocal(small[:, 88:96], small[:, 80:88]))
            x = PS[:, bank, :].rearrange("p (h d) -> p h d", h=8)
            for t in range(NT):
                done(eng.tensor_tensor(dst[:, t], x[:, 4 * t:4 * t + 4, :],
                                       small[:, 88 + 4 * t:92 + 4 * t].unsqueeze(2).to_broadcast([P, 4, DH]),
                                       ALU.mult))
            for t in range(NT):
                done(eng.tensor_tensor(dst[:, t], dst[:, t], gain_row.unsqueeze(1).to_broadcast([P, 4, DH]),
                                       ALU.mult), ready if t == NT - 1 else None)

        def dve_rope(done, x, n_heads, tmp, ready):
            eng = done.eng
            n = n_heads * ROPE_HALF
            ta, tb, tc, td = (tmp[:, i * n:(i + 1) * n].rearrange("p (h r) -> p h r", h=n_heads) for i in range(4))
            for t in range(NT):
                x1, x2 = x[:, t, :, 0:ROPE_HALF], x[:, t, :, ROPE_HALF:2 * ROPE_HALF]
                c = cos_t[:, t, :].unsqueeze(1).to_broadcast([P, n_heads, ROPE_HALF])
                s = sin_t[:, t, :].unsqueeze(1).to_broadcast([P, n_heads, ROPE_HALF])
                done(eng.tensor_tensor(ta, x1, c, ALU.mult))
                done(eng.tensor_tensor(tb, x2, s, ALU.mult))
                done(eng.tensor_tensor(tc, x2, c, ALU.mult))
                done(eng.tensor_tensor(td, x1, s, ALU.mult))
                done(eng.tensor_tensor(x1, ta, tb, ALU.subtract))
                done(eng.tensor_tensor(x2, tc, td, ALU.add), ready if t == NT - 1 else None)

        OUT = [PS[:, 0:2, :].rearrange("p b c -> p (b c)"), PS[:, 2:4, :].rearrange("p b c -> p (b c)")]
        GATHER, GU, Y0 = 4, 5, 6

        def gu_view(i):
            return PS[:, GU, i * PASS:(i + 1) * PASS]

        def pe_gather(pe_, hot):
            for k in range(KC):
                for t in range(NT):
                    mm = pe_.matmul(PS[:, GATHER, k * PASS:(k + 1) * PASS], u[:, t, k * P:(k + 1) * P],
                                    hot[:, t, :], start=(t == 0), stop=(t == NT - 1))
            return mm

        def pe_gate_up(pe_, n, x):
            for i in range(4):
                w = slot(n + i // 2)
                for k in range(KC):
                    mm = pe_.matmul(gu_view(i), w[:, k, (i % 2) * P:(i % 2 + 1) * P], x[:, k, :],
                                    start=(k == 0), stop=(k == KC - 1))
            return mm

        def pe_down(pe_, n, rows, half):
            w = slot(n + 2, 2)
            for j in range(2):
                mm = pe_.matmul(PS[rows:rows + PASS, Y0 + half, :], hid[:, j, :], w[:, j, half * 512:(half + 1) * 512],
                                start=(j == 0), stop=(j == 1))
            return mm

        def pe_turn_weights(pe_, width_):
            for t in range(NT):
                mm = pe_.transpose(PS[0:width_, GU, 256 + t * P:256 + (t + 1) * P], hot_w[:, t, 0:width_], ident[:, :])
            return mm

        def pe_combine(pe_, rows, half):
            for t in range(NT):
                mm = pe_.matmul(OUT[t][:, half * 512:(half + 1) * 512], hot_wT[0:rows, t * P:(t + 1) * P],
                                y_rows[0:rows, half * 512:(half + 1) * 512], start=False, stop=False,
                                skip_group_check=True)
            return mm

        def table(eng, row, e):
            return eng.value_load(passes_i[0:1, row, bass.ds(e, 1)], min_val=0,
                                  max_val=MAX_PASSES - 1 if row == 0 else SEQ)

        def more_passes(eng, e, body):
            n = table(eng, 0, e)
            with eng.If(n > 0):
                first = table(eng, 1, e)
                with eng.Fori(0, n) as k:
                    body(first + k, k)

        def pe_moe(pe_, layer):
            m = moe_sem[layer]
            n_sh, n_ex = U_SHARED[layer], U_EXPERTS[layer]
            tag = f"ffn{layer}"
            pe_turn_rows(pe_, u, (rows_modulated, 2 * MODULATED.index(tag) + 2), tag)
            pe_.wait_ge(router_loaded, 16 * (layer + 1))
            for t in range(NT):
                for k in range(KC):
                    mm = pe_.matmul(PS[:, Y0, t * N_EXP:(t + 1) * N_EXP], uT[:, k, t * P:(t + 1) * P],
                                    w_router[:, k, :], start=(k == 0), stop=(k == KC - 1))
            mm.then_inc(m["router_out"], 1)
            for i in range(4):
                landed(pe_, n_sh + i // 2)
                for k in range(KC):
                    mm = pe_.matmul(PS[:, 4 + i // 2, (i % 2) * SEQ:(i % 2 + 1) * SEQ],
                                    slot(n_sh + i // 2)[:, k, (i % 2) * P:(i % 2 + 1) * P], uT[:, k, :],
                                    start=(k == 0), stop=(k == KC - 1))
                if i % 2:
                    mm.then_inc(unit_done, 1)
            pe_.wait_ge(m["mask_ready"], 1)
            R = PS[:, Y0 + 1, 0:NT * N_EXP].rearrange("p (t e) -> p t e", t=NT)
            pe_.matmul(R[:, 0, :], before[:, :], routed[:, 0, :], start=True, stop=True).then_inc(m["more_added"], 1)
            pe_.matmul(R[:, 1, :], ones[:, :], routed[:, 0, :], start=True, stop=False)
            pe_.matmul(R[:, 1, :], before[:, :], routed[:, 1, :], start=False, stop=True)
            lengths = PS[0:N_EXP, Y0 + 1, 256:256 + P]
            for t in range(NT):
                mm = pe_.matmul(lengths, routed[:, t, :], ones[:, :], start=(t == 0), stop=(t == NT - 1))
            mm.then_inc(m["ranks_out"], 1)
            pe_.wait_ge(m["shared_hid"], 1)
            landed(pe_, n_sh + 2)
            for t in range(NT):
                for half in range(2):
                    for j in range(2):
                        mm = pe_.matmul(OUT[t][:, half * 512:(half + 1) * 512], sh_hid[:, j, t * P:(t + 1) * P],
                                        slot(n_sh + 2, 2)[:, j, half * 512:(half + 1) * 512],
                                        start=(j == 0), stop=(j == 1))
            mm.then_inc(unit_done, 1)
            pe_.wait_ge(m["passes_ready"], 1)
            tables = PS[:, Y0, 128:128 + 2 * TABLE].rearrange("p (a e) -> p a e", a=2)
            pe_.matmul(tables[:, 0, 0:N_EXP], passes_f[0:N_EXP, :], ident[0:N_EXP, 0:N_EXP], start=True, stop=True)
            mm = pe_.matmul(tables[:, 1, :], passes_f[0:N_EXP, :], before[0:N_EXP, 0:TABLE], start=True, stop=True)
            mm.then_inc(m["passes_out"], 1)
            pe_.wait_ge(m["onehot_ready"], 2)
            pe_gather(pe_, one_hot[0]).then_inc(m["gathered"], 1)
            pe_.wait_ge(m["tables_ready"], 1)

            with pe_.Fori(0, TURNS) as turn:
                for q in range(BODY // 2):
                    for x in range(2):
                        r = 2 * q + x
                        e = turn * BODY + r
                        n = n_ex + 3 * r
                        pe_.wait_ge(m["x_ready"], e + 1)
                        for i in range(2):
                            pe_.wait_ge(slot_loaded[(n + i) % SLOTS], 16 * ((n + i) // SLOTS + 1) + turn * 16)
                        pe_gate_up(pe_, n, x_exp).then_inc(m["gu_out"], 1)
                        pe_.wait_ge(m["onehot_ready"], e * 2 + 4)
                        pe_gather(pe_, one_hot[(r + 1) % 2]).then_inc(m["gathered"], 1)
                        pe_.wait_ge(slot_loaded[(n + 2) % SLOTS], 16 * ((n + 2) // SLOTS + 1) + turn * 16)
                        if x == 1:
                            pe_.wait_ge(m["hot_w_ready"], (turn * 2 + q + 1) * 4)
                            pe_.wait_ge(m["hid_ready"], e + 1)
                            pe_turn_weights(pe_, 2 * PASS).then_inc(m["hot_w_turned"], 1)
                            pe_down(pe_, n, PASS, 0).then_inc(m["y_out"], 1)
                            pe_down(pe_, n, PASS, 1).then_inc(m["y_out"], 1)
                        else:
                            pe_.wait_ge(m["hid_ready"], e + 1)
                            pe_down(pe_, n, 0, 0)
                            pe_down(pe_, n, 0, 1)
                    pair = turn * 2 + q
                    pe_.wait_ge(m["hot_wT_ready"], pair + 1)
                    pe_.wait_ge(m["y_ready"], pair * 2 + 1)
                    pe_combine(pe_, 2 * PASS, 0)
                    pe_.wait_ge(m["y_ready"], pair * 2 + 2)
                    pe_combine(pe_, 2 * PASS, 1).then_inc(unit_done, 6)
                    pe_.wait_ge(m["x_ready"], pair * 2 + 3)
                    for x in range(2):
                        r = 2 * q + x
                        n = n_ex + 3 * r

                        def one_more(i, k, n=n):
                            pe_.wait_ge(m["more_onehot"], i * 4 + 4)
                            pe_gather(pe_, hot_more).then_inc(m["more_gathered"], 1)
                            pe_turn_weights(pe_, PASS).then_inc(m["more_turned"], 1)
                            pe_.wait_ge(m["more_x"], i + 1)
                            pe_.wait_ge(m["more_wT"], i + 1)
                            pe_gate_up(pe_, n, x_more).then_inc(m["more_gu"], 1)
                            pe_.wait_ge(m["more_hid"], i + 1)
                            pe_down(pe_, n, 0, 0)
                            pe_down(pe_, n, 0, 1).then_inc(m["more_y_out"], 1)
                            pe_.wait_ge(m["more_y"], i * 2 + 2)
                            pe_combine(pe_, PASS, 0)
                            pe_combine(pe_, PASS, 1).then_inc(m["more_added"], 1)

                        more_passes(pe_, turn * BODY + r, one_more)

        def act_moe(done, layer):
            act, m = done.eng, moe_sem[layer]
            tag = f"ffn{layer}"
            act_row_norms(done, tag, (mix_added, 4 * layer + 4))
            act_copy_turned(done, uT, tag)
            act.wait_ge(m["router_out"], 1)
            done(act.activation(scores.rearrange("p t e -> p (t e)"), PS[:, Y0, 0:NT * N_EXP], ACT.Sigmoid),
                 m["scores_ready"])
            act.wait_ge(unit_done, U_SHARED[layer] + 1)
            done(act.activation(sh_act.rearrange("p j t -> p (j t)"), PS[:, 4, :], ACT.Silu), m["shared_act"])
            act.wait_ge(m["gathered"], 1)
            done(act.activation(x_exp.rearrange("p k s -> p (k s)"), PS[:, GATHER, :], ACT.Copy), m["x_ready"])
            act.wait_ge(m["tables_ready"], 1)
            with act.Fori(0, TURNS) as turn:
                for q in range(BODY // 2):
                    pair = turn * 2 + q
                    for x in range(2):
                        e = turn * BODY + (2 * q + x)
                        act.wait_ge(m["gu_out"], e + 1)
                        act.activation(gate_act.rearrange("p j s -> p (j s)"), PS[:, GU, 0:2 * PASS],
                                       ACT.Silu).then_inc(m["gate_ready"], 1)
                        act.wait_ge(m["gathered"], e + 2)
                        act.activation(x_exp.rearrange("p k s -> p (k s)"), PS[:, GATHER, :],
                                       ACT.Copy).then_inc(m["x_ready"], 1)
                    act.wait_ge(m["hot_w_turned"], pair + 1)
                    act.activation(hot_wT, PS[:, GU, 256:512], ACT.Copy).then_inc(m["hot_wT_ready"], 1)
                    for x in range(2):
                        def one_more(i, k):
                            act.wait_ge(m["more_gathered"], i + 1)
                            act.activation(x_more.rearrange("p k s -> p (k s)"), PS[:, GATHER, :],
                                           ACT.Copy).then_inc(m["more_x"], 1)
                            act.wait_ge(m["more_turned"], i + 1)
                            act.activation(hot_wT[0:PASS, :], PS[0:PASS, GU, 256:512],
                                           ACT.Copy).then_inc(m["more_wT"], 1)
                            act.wait_ge(m["more_gu"], i + 1)
                            act.activation(gate_act.rearrange("p j s -> p (j s)"), PS[:, GU, 0:2 * PASS],
                                           ACT.Silu).then_inc(m["more_gate"], 1)

                        more_passes(act, turn * BODY + (2 * q + x), one_more)

        def dve_moe(done, layer):
            dve, m = done.eng, moe_sem[layer]
            tag = f"ffn{layer}"
            dve_row_norms(done, tag)
            dve_modulate(done, ada[:, SH_F, :], ada[:, SC_F, :], [1, 4][layer], True, rows_modulated)
            done(dve.memset(slot_of[:, :, :], -1.0))
            done(dve.memset(weight_of[:, :, :], 0.0))
            done(dve.memset(passes_i[:, :, :], 0))
            dve.wait_ge(m["scores_ready"], 1)
            for t in range(NT):
                done(dve.tensor_tensor(chosen_by[:, t, :], scores[:, t, :], bias_router[:, layer, :], ALU.add))
                done(dve.max(top8[:, t, :], chosen_by[:, t, :]))
                done(dve.match_replace(replaced[:, t, :], top8[:, t, :], chosen_by[:, t, :], MASKED))
            done(dve.tensor_tensor(routed, replaced, chosen_by, ALU.not_equal), m["mask_ready"])
            done(dve.tensor_tensor(scores, scores, routed, ALU.mult))
            done(dve.tensor_reduce(rsum, scores, AX.X, ALU.add))
            done(dve.reciprocal(rsum, rsum))
            for t in range(NT):
                done(dve.tensor_scalar(weight_of[:, t, 0:N_EXP], scores[:, t, :], rsum[:, t:t + 1], ROUTED_SCALE,
                                       ALU.mult, ALU.mult))
            dve.wait_ge(m["ranks_out"], 1)
            R = PS[:, Y0 + 1, 0:NT * N_EXP].rearrange("p (t e) -> p t e", t=NT)
            done(dve.scalar_tensor_tensor(out=slot_of[:, :, 0:N_EXP], in0=R, scalar=1.0, in1=routed,
                                          op0=ALU.add, op1=ALU.mult))
            done(dve.tensor_scalar(slot_of[:, :, 0:N_EXP], slot_of[:, :, 0:N_EXP], -1.0, None, ALU.add))
            lengths = PS[0:N_EXP, Y0 + 1, 256:256 + P]
            pf = passes_f[0:N_EXP, :]
            done(dve.tensor_scalar(pf, lengths, float(PASS), None, ALU.is_gt))
            for i in range(2, MAX_PASSES):
                done(dve.scalar_tensor_tensor(out=pf, in0=lengths, scalar=float(i * PASS), in1=pf,
                                              op0=ALU.is_gt, op1=ALU.add),
                     m["passes_ready"] if i == MAX_PASSES - 1 else None)

            def hot(dst, t, e, first=0):
                return dve.tensor_scalar(dst[:, t, :], iota[:, bass.ds(first, PASS)], slot_of[:, t, bass.ds(e, 1)],
                                         None, ALU.is_equal)

            def hot_weighted(t, at, e, first=0):
                return dve.tensor_scalar(hot_w[:, t, at:at + PASS], iota[:, bass.ds(first, PASS)],
                                         slot_of[:, t, bass.ds(e, 1)], weight_of[:, t, bass.ds(e, 1)],
                                         ALU.is_equal, ALU.mult)

            for t in range(NT):
                done(hot(one_hot[0], t, 0), m["onehot_ready"])
            dve.wait_ge(unit_done, U_SHARED[layer] + 2)
            dve.wait_ge(m["shared_act"], 1)
            done(dve.tensor_tensor(sh_hid.rearrange("p j t -> p (j t)"), sh_act.rearrange("p j t -> p (j t)"),
                                   PS[:, 5, :], ALU.mult), m["shared_hid"])
            for t in range(NT):
                done(hot(one_hot[1], t, 1), m["onehot_ready"])
            dve.wait_ge(m["passes_out"], 1)
            tables = PS[0:1, Y0, 128:128 + 2 * TABLE].rearrange("p (a e) -> p a e", a=2)
            done(dve.tensor_copy(passes_i[:, 0, 0:N_EXP], tables[:, 0, 0:N_EXP]))
            done(dve.tensor_copy(passes_i[:, 1, :], tables[:, 1, :]), m["tables_ready"])

            with dve.Fori(0, TURNS) as turn:
                for q in range(BODY // 2):
                    pair = turn * 2 + q
                    for x in range(2):
                        r = 2 * q + x
                        e = turn * BODY + r
                        dve.wait_ge(m["gate_ready"], e + 1)
                        dve.tensor_tensor(hid.rearrange("p j s -> p (j s)"),
                                          gate_act.rearrange("p j s -> p (j s)"),
                                          PS[:, GU, 2 * PASS:4 * PASS], ALU.mult).then_inc(m["hid_ready"], 1)
                        for t in range(NT):
                            hot(one_hot[r % 2], t, e + 2).then_inc(m["onehot_ready"], 1)
                        if x == 0:
                            for y in range(2):
                                for t in range(NT):
                                    hot_weighted(t, y * PASS, e + y).then_inc(m["hot_w_ready"], 1)
                    for half in range(2):
                        dve.wait_ge(m["y_out"], pair * 2 + half + 1)
                        dve.tensor_copy(y_rows[:, half * 512:(half + 1) * 512],
                                        PS[:, Y0 + half, :]).then_inc(m["y_ready"], 1)
                    for x in range(2):
                        e_ = turn * BODY + (2 * q + x)

                        def one_more(i, k, e_=e_):
                            for t in range(NT):
                                hot(hot_more, t, e_, (k + 1) * PASS).then_inc(m["more_onehot"], 1)
                                hot_weighted(t, 0, e_, (k + 1) * PASS).then_inc(m["more_onehot"], 1)
                            dve.wait_ge(m["more_gate"], i + 1)
                            dve.tensor_tensor(hid.rearrange("p j s -> p (j s)"),
                                              gate_act.rearrange("p j s -> p (j s)"),
                                              PS[:, GU, 2 * PASS:4 * PASS], ALU.mult).then_inc(m["more_hid"], 1)
                            dve.wait_ge(m["more_y_out"], i + 1)
                            for half in range(2):
                                dve.tensor_copy(y_rows[0:PASS, half * 512:(half + 1) * 512],
                                                PS[0:PASS, Y0 + half, :]).then_inc(m["more_y"], 1)

                        more_passes(dve, e_, one_more)
            dve.wait_ge(unit_done, U_EXPERTS[layer] + 3 * N_EXP)
            dve.wait_ge(m["x_ready"], N_EXP + 1)
            total = table(dve, 1, N_EXP)
            dve.wait_ge(m["more_added"], total + 1)
            for t in range(NT):
                done(dve.tensor_tensor(g_tmp, OUT[t], ada[:, G_F, :], ALU.mult))
                done(dve.tensor_tensor(h[:, t, :], h[:, t, :], g_tmp, ALU.add),
                     layer_added)

        block = ctx.enter_context(nc.Block())

        @block.sync
        def _(sp):
            def load(n, src, k=KC, ready=None):
                if n >= SLOTS:
                    sp.wait_ge(unit_done, n - SLOTS + 1)
                sp.dma_start(slot(n, k), src).then_inc(slot_loaded[n % SLOTS], 16)

            def columns(n0, w, n):
                for j in range(n):
                    load(n0 + j, w[:, j * UC:(j + 1) * UC].rearrange("(k p) c -> p k c", p=P))

            def wide(w):
                return w.rearrange("(p k) c -> p k c", k=KC)

            def tall(w):
                return w.rearrange("(j p) c -> p j c", p=P)

            def experts(layer):
                n0 = U_EXPERTS[layer]
                m = moe_sem[layer]
                names = ("w_exp_gate", "w_exp_up", "w_exp_down")

                def fetch(r, src):
                    n = n0 + 3 * r
                    for i in range(3):
                        s = (n + i) % SLOTS
                        sp.dma_start(slot(n + i, 2 if i == 2 else KC), src(i)).then_inc(slot_loaded[s], 16)

                for r in range(BODY):
                    for i in range(3):
                        load(n0 + 3 * r + i, (tall if i == 2 else wide)(a[names[i]][layer, r]), 2 if i == 2 else KC)
                sp.wait_ge(m["tables_ready"], 1)
                with sp.Fori(1, TURNS) as turn:
                    for q in range(BODY // 2):
                        sp.wait_ge(unit_done, turn * SLOTS + (n0 + 6 * q - SLOTS + 6))
                        upto_pair = table(sp, 1, turn * BODY + (2 * q + 2 - BODY))
                        sp.wait_ge(m["more_added"], upto_pair + 1)
                        for x in range(2):
                            r = 2 * q + x

                            def src(i):
                                w = a[names[i]][layer, bass.ds(turn * BODY + r, 1), :, :]
                                if i == 2:
                                    return w.rearrange("o (j p) c -> p (o j) c", p=P)
                                return w.rearrange("o (p k) c -> p (o k) c", k=KC)

                            fetch(r, src)

            columns(U_ADA[0], a["w_ada"][0], 24)
            columns(U_QKV, a["w_in_a"][0], 12)
            columns(U_OUT_A, a["w_o_a"][0], 4)
            load(U_SHARED[0], wide(a["w_sh_gate"][0]))
            load(U_SHARED[0] + 1, wide(a["w_sh_up"][0]))
            load(U_SHARED[0] + 2, tall(a["w_sh_down"][0]), 2)
            experts(0)
            for q in range(BODY // 2):
                upto_pair = table(sp, 1, N_EXP - BODY + 2 * q + 2)
                sp.wait_ge(unit_done, U_ADA[1] - SLOTS + 6 * q + 6)
                sp.wait_ge(moe_sem[0]["more_added"], upto_pair + 1)
                for j in range(6 * q, 6 * q + 6):
                    load(U_ADA[1] + j, a["w_ada"][1][:, j * UC:(j + 1) * UC].rearrange("(k p) c -> p k c", p=P))
            for j in range(12, 24):
                load(U_ADA[1] + j, a["w_ada"][1][:, j * UC:(j + 1) * UC].rearrange("(k p) c -> p k c", p=P))
            columns(U_ADA_KV, a["w_ada_kv"], 8)
            columns(U_KV, a["w_kv_b"], 6)
            for c, name in enumerate(("w_cmp_k1", "w_cmp_v1")):
                for j in range(4):
                    load(U_CMP + 4 * c + j, a[name][j * D:(j + 1) * D, :].rearrange("(k p) c -> p k c", p=P))
            columns(U_Q, a["w_in_b"][0], 4)
            columns(U_OUT_B, a["w_o_b"][0], 4)
            load(U_SHARED[1], wide(a["w_sh_gate"][1]))
            load(U_SHARED[1] + 1, wide(a["w_sh_up"][1]))
            load(U_SHARED[1] + 2, tall(a["w_sh_down"][1]), 2)
            experts(1)
            for t in range(NT):
                sp.wait_ge(layer_added, NT + t + 1)
                sp.dma_start(out[0, t * P:(t + 1) * P, :], h[:, t, :]).then_inc(stored, 16)
            sp.wait_ge(stored, 16 * NT)

        @block.gpsimd
        def _(pool):
            def rows(name_ap):
                return name_ap.partition_broadcast(P)

            pool.dma_start(cond[:, :], a["c"].rearrange("o (k p) -> p (o k)", p=P),
                           allow_slow_non_contiguous=True).then_inc(params, 16)
            pool.dma_start(pos_i[:, :], a["positions"].rearrange("o (t p) -> p (o t)", p=P),
                           allow_slow_non_contiguous=True).then_inc(params, 16)
            for t in range(NT):
                pool.dma_start(h[:, t, :], a["x"][0, t * P:(t + 1) * P, :]).then_inc(x_loaded, 16)
            pool.dma_start(ada[:, :, :].rearrange("p a d -> p (a d)"), rows(a["b_ada"][0])).then_inc(bias_loaded, 16)
            pool.dma_start(gain[:, :], rows(a["norm_mix"][0])).then_inc(gain_loaded, 16)
            for dst, src in ((gain_qa, "qnorm_a"), (gain_ka, "knorm_a"), (gain_qb, "qnorm_b"),
                             (bias_f, "b_f_a"), (bias_gate, "b_gate_b")):
                pool.dma_start(dst[:, :], rows(a[src][0])).then_inc(params, 16)
            for i in range(3):
                pool.dma_start(gain_kb[:, i, :], rows(a["knorm_b"][i])).then_inc(params, 16)
            for i in range(2):
                pool.dma_start(bias_router[:, i, :], rows(a["b_router"][i])).then_inc(params, 16)
            for i, name in enumerate(("pe_cmp_k", "pe_cmp_v")):
                for half in range(2):
                    pool.dma_start(pe[half * CMP:(half + 1) * CMP, i, :], a[name]).then_inc(params, 16)
            pool.dma_start(w_forget, a["w_in_a"][0][:, 3 * D:3 * D + H].rearrange("(k p) c -> p k c", p=P)
                           ).then_inc(params, 16)
            done = Steps(pool, pool_step)
            done(pool.memset(ident[:, :], 0.0))
            done(pool.memset(ones[:, :], 1.0))
            done(pool.memset(causal[:, :], 0.0))
            done(pool.memset(upto[:, :], 1.0))
            done(pool.memset(before[:, :], 1.0))
            done(pool.memset(block_diag[:, :], 1.0))
            done(pool.affine_select(out=ident[:, :], in_=ident[:, :], compare_op=ALU.not_equal, fill=1.0,
                                    base=0, pattern=[[-1, P]], channel_multiplier=1))
            done(pool.affine_select(out=upto[:, :], in_=upto[:, :], compare_op=ALU.is_ge, fill=0.0,
                                    base=0, pattern=[[1, P]], channel_multiplier=-1))
            done(pool.affine_select(out=before[:, :], in_=before[:, :], compare_op=ALU.is_ge, fill=0.0,
                                    base=-1, pattern=[[1, P]], channel_multiplier=-1))
            done(pool.affine_select(out=causal[:, P:2 * P], in_=causal[:, P:2 * P], compare_op=ALU.is_ge,
                                    fill=MASKED, base=0, pattern=[[-1, P]], channel_multiplier=1))
            done(pool.affine_select(out=block_diag[:, :], in_=block_diag[:, :], compare_op=ALU.is_ge, fill=0.0,
                                    base=0, pattern=[[-NB, H]], channel_multiplier=1))
            done(pool.affine_select(out=block_diag[:, :], in_=block_diag[:, :], compare_op=ALU.is_ge, fill=0.0,
                                    base=NB - 1, pattern=[[NB, H]], channel_multiplier=-1))
            for i in range(ROPE_HALF):
                f = np.float32(ROPE_THETA) ** np.float32(-2 * i / (2 * ROPE_HALF))
                done(pool.memset(freq[:, i:i + 1], float(f)))
            done(pool.iota(partition_no[:, :], pattern=[[0, 1]], base=0, channel_multiplier=1,
                           allow_small_or_imprecise_dtypes=True))
            done(pool.iota(iota[:, :], pattern=[[1, SEQ]], base=0, channel_multiplier=0,
                           allow_small_or_imprecise_dtypes=True), consts)
            for i, src in enumerate((a["norm_ffn"][0], a["norm_kv"], a["norm_mix"][1], a["norm_ffn"][1])):
                pool.wait_ge(gain_used, i + 1)
                pool.dma_start(gain[:, :], rows(src)).then_inc(gain_loaded, 16)
                if i in (0, 3):
                    layer = i // 3
                    pool.wait_ge(mix_added, 4 * layer + 4)
                    pool.dma_start(w_router, a["w_router"][layer].rearrange("(p k) c -> p k c", k=KC)
                                   ).then_inc(router_loaded, 16)
                if i == 0:
                    pool.dma_start(w_gates[:, :, :], a["w_in_b"][0][:, D:D + 3 * H].rearrange(
                        "(k p) c -> p k c", p=P)).then_inc(nsa_params, 16)
                    pool.wait_ge(layer_added, NT)
                    for c, name in enumerate(("w_cmp_k2", "w_cmp_v2")):
                        pool.dma_start(w_cmp2[:, c, :, :], a[name].rearrange("(j p) c -> p j c", p=P)
                                       ).then_inc(nsa_params, 16)
                    pool.dma_start(ada[:, :, :].rearrange("p a d -> p (a d)"), rows(a["b_ada"][1])
                                   ).then_inc(bias_loaded, 16)
                    pool.dma_start(ada_kv.rearrange("p a d -> p (a d)"), rows(a["b_ada_kv"])
                                   ).then_inc(bias_kv_loaded, 16)

        N_PARAMS = 2 + 5 + 3 + 2 + 4 + 1
        fox_batches = attention_batches("fox")
        nsa_batches = attention_batches("nsa")

        @block.tensor
        def _(pe_):
            pe_.wait_ge(consts, 1)
            pe_.wait_ge(cond_ready, 2)
            pe_ada(pe_, U_ADA[0], 24, 0)

            pe_.wait_ge(ada_read, 24)
            pe_turn_rows(pe_, u, (rows_modulated, 2 * MODULATED.index("mix0") + 2), "mix0")

            def turn_unit(j):
                pe_.wait_ge(sem("fox_normed"), j + 1)
                if j >= 2:
                    pe_.wait_ge(sem("fox_copied"), j - 1 if j - 2 < 4 else 4 + 2 * (j - 2 - 3))
                src = normed[j % 2].rearrange("p (t c) -> p t c", t=NT)
                for c in range(2):
                    for t in range(NT):
                        mm = pe_.transpose(PS[:, 4 + j % 2, c * SEQ + t * P:c * SEQ + (t + 1) * P],
                                           src[:, t, c * P:(c + 1) * P], ident[:, :])
                mm.then_inc(sem("fox_turned"), 1)

            for j in range(12):
                if j >= 4:
                    if j - 4 < 8:
                        pe_.wait_ge(sem("fox_normed"), j - 3)
                pe_rows_unit(pe_, U_QKV + j, j % 4, uT)
                if 1 <= j <= 8:
                    turn_unit(j - 1)
            pe_.wait_ge(params, 16 * N_PARAMS)
            for t in range(NT):
                for k in range(KC):
                    mm = pe_.matmul(PS[:, 6, t * H:(t + 1) * H], uT[:, k, t * P:(t + 1) * P], w_forget[:, k, :],
                                    start=(k == 0), stop=(k == KC - 1))
            mm.then_inc(sem("forget_out"), 1)
            lf = fg[4].rearrange("p (t h) -> p t h", t=NT)
            pe_.wait_ge(sem("logf_ready"), 1)
            pe_.matmul(PS[:, 7, 0:H], upto[:, :], lf[:, 0, :], start=True, stop=True)
            pe_.matmul(PS[:, 7, H:2 * H], ones[:, :], lf[:, 0, :], start=True, stop=False)
            pe_.matmul(PS[:, 7, H:2 * H], upto[:, :], lf[:, 1, :], start=False, stop=True).then_inc(sem("cum_out"), 1)
            pe_.wait_ge(sem("cum_ready"), 1)
            for t in range(NT):
                mm = pe_.transpose(PS[:, 6, t * P:(t + 1) * P], cum[:, t, :], ident[:, :])
            mm.then_inc(sem("cum_turned"), 1)
            pe_.wait_ge(sem("cumT_ready"), 1)
            pe_.wait_ge(sem("fox_copied"), 12)
            pe_.wait_ge(sem("fox_v"), 4)
            pe_attention(pe_, "fox", fox_batches, lambda br, hd: kz_a[:, hd, :],
                         lambda br, kt, hd: v_a[:, kt, hd * DH:(hd + 1) * DH])
            pe_turn_rows(pe_, u, (heads_read, 8), "fox_o")
            for j in range(4):
                pe_rows_unit(pe_, U_OUT_A + j, 4 + j, uT)
            pe_.wait_ge(mix_added, 4)
            pe_moe(pe_, 0)

            pe_.wait_ge(layer_added, NT)
            pe_.wait_ge(cond_ready, 3)
            pe_ada(pe_, U_ADA[1], 24, 24)
            pe_.wait_ge(ada_read, 48)
            pe_ada(pe_, U_ADA_KV, 8, 48)
            pe_.wait_ge(ada_read, 56)
            pe_turn_rows(pe_, u, (rows_modulated, 2 * MODULATED.index("kv") + 2), "kv")
            for j in range(6):
                if j >= 4:
                    pe_.wait_ge(sem("kv_doubled"), j - 3)
                pe_rows_unit(pe_, U_KV + j, j % 4, uT)
            for i in range(4):
                pe_.wait_ge(sem("kv_doubled"), i + 1)
                if i >= 1:
                    pe_.wait_ge(sem("kv_copied"), [0, 8, 16, 18][i])
                for g in range(G):
                    for t in range(NT):
                        mm = pe_.transpose(PS[:, 4 + g // 2, (g % 2) * SEQ + t * P:(g % 2) * SEQ + (t + 1) * P],
                                           doubled[i % 2][:, t, g].rearrange("p a d -> p (a d)"), ident[:, :])
                mm.then_inc(sem("kv_turned2"), 1)
            pe_.wait_ge(sem("kv_copied"), 20)
            pe_.wait_ge(nsa_params, 16 * 3)
            for c in range(2):
                if c == 1:
                    pe_.wait_ge(sem("cmp_hidden"), 2)
                for j in range(4):
                    n = U_CMP + 4 * c + j
                    landed(pe_, n)
                    for k in range(KC):
                        for i in range(2):
                            mm = pe_.matmul(PS[:, 4 + i, 0:G * NB], slot(n)[:, k, i * P:(i + 1) * P],
                                            flat[c][:, KC * j + k, :], start=(j + k == 0), stop=(j == 3 and k == 7))
                    mm.then_inc(unit_done, 1)
                if c == 0:
                    pe_.wait_ge(sem("cmp_hidden"), 2)
                    for i in range(2):
                        mm = pe_.matmul(PS[0:G * NB, 6, 0:DH], hidden[:, i, :], w_cmp2[:, 0, i, :],
                                        start=(i == 0), stop=(i == 1))
                    mm.then_inc(sem("cmp_k"), 1)
                    pe_.wait_ge(sem("cmp_k_normed"), 1)
                    pe_.transpose(PS[:, 6, 0:G * NB], kc_rows[0:G * NB].rearrange("p a d -> p (a d)"),
                                  ident[0:G * NB, 0:G * NB]).then_inc(sem("cmp_k_turned"), 1)
                else:
                    pe_.wait_ge(sem("cmp_rep"), 2)
                    for i in range(2):
                        mm = pe_.matmul(PS[0:H * NB, 7, 0:DH], hidden_rep[:, i, :], w_cmp2[:, 1, i, :],
                                        start=(i == 0), stop=(i == 1))
                    mm.then_inc(sem("cmp_v"), 1)
            pe_turn_rows(pe_, u, (rows_modulated, 2 * MODULATED.index("mix1") + 2), "mix1",
                         [(sem("kv_doubled"), 4), (sem("kv_values"), 2), (sem("kcz_ready"), 2)])
            for t in range(NT):
                for k in range(KC):
                    mm = pe_.matmul(PS[:, 6, t * 3 * H:(t + 1) * 3 * H], uT[:, k, t * P:(t + 1) * P],
                                    w_gates[:, k, :], start=(k == 0), stop=(k == KC - 1))
            mm.then_inc(sem("gates_out"), 1)
            for j in range(4):
                pe_rows_unit(pe_, U_Q + j, j, uT)
            pe_turn_rows(pe_, q_rows, (sem("q_normed"), 4), "q")
            pe_.wait_ge(sem("gates_ready"), 1)
            for t in range(NT):
                for hd in range(H):
                    g = hd // HPG
                    mm = pe_.matmul(PS[:, 6, t * H * NB + hd * NB:t * H * NB + (hd + 1) * NB],
                                    qT[:, hd // 2, t * P:(t + 1) * P], kcz[:, hd % 2, g * NB:(g + 1) * NB],
                                    start=True, stop=True)
            mm.then_inc(sem("cmp_logits"), 1)
            pe_.wait_ge(sem("cmp_probs"), NT)
            for t in range(NT):
                mm = pe_.transpose(PS[0:H * NB, 7, t * P:(t + 1) * P], cmp_buf[:, t, :], ident[:, :])
            mm.then_inc(sem("cmp_probs_turned"), 1)
            pe_.wait_ge(sem("cmp_probsT"), 1)
            for t in range(NT):
                for half in range(2):
                    pe_.matmul(PS[:, 2 * t + half, :], cmp_T[0:H * NB, t * P:(t + 1) * P],
                               v_diag[0:H * NB, 8 * half:8 * half + 8, :].rearrange("p h d -> p (h d)"),
                               start=True, stop=True).then_inc(sem("cmp_heads"), 1)
            pe_.wait_ge(sem("cmp_heads_read"), 2)
            pe_turn_rows(pe_, q_rows, (sem("q_rotated"), 1), "q_rotated")
            pe_attention(pe_, "nsa", nsa_batches, lambda br, hd: kz_b[:, br, hd // HPG, hd % 2, :],
                         lambda br, kt, hd: v_b[:, br, kt, (hd // HPG) * DH:(hd // HPG + 1) * DH])
            pe_turn_rows(pe_, u, (sem("nsa_o"), 16), "nsa_o")
            for j in range(4):
                pe_rows_unit(pe_, U_OUT_B + j, 4 + j, uT)
            pe_.wait_ge(mix_added, 8)
            pe_moe(pe_, 1)

        @block.scalar
        def _(act):
            done = Steps(act, act_step)
            act.wait_ge(params, 16 * N_PARAMS)
            done(act.activation(cond[:, :], cond[:, :], ACT.Silu), cond_ready)
            act.wait_ge(sem("angles"), 2)
            done(act.activation(sin_t[:, :, :], sin_t[:, :, :], ACT.Sin))
            done(act.activation(cos_t[:, :, :], cos_t[:, :, :], ACT.Sin), sem("rope_ready"))
            act_row_norms(done, "mix0", (x_loaded, 16 * NT))
            act_copy_turned(done, uT, "mix0")
            copied = sem("fox_copied")

            def copy_unit(j):
                act.wait_ge(sem("fox_turned"), j + 1)
                src = PS[:, 4 + j % 2, :].rearrange("p (c t) -> p c t", c=2)
                if j < 4:
                    done(act.activation(qT[:, 2 * j:2 * j + 2, :], src, ACT.Copy), copied)
                else:
                    hd = 4 * (j - 4)
                    for par in range(2):
                        rows = slice(par * DH, (par + 1) * DH)
                        done(act.activation(kz_a[rows, hd + par:hd + 4:2, :], src[rows], ACT.Copy), copied)

            act.wait_ge(sem("kz_zeroed"), 1)
            for j in range(8):
                act_head_squares(done, "foxn", j, U_QKV + j, j % 4)
                if j >= 1:
                    copy_unit(j - 1)
            copy_unit(7)
            for j in range(4):
                act.wait_ge(unit_done, U_QKV + 8 + j + 1)
                done(act.activation(v_a[:, :, j * UC:(j + 1) * UC],
                                    PS[:, j % 4, :].rearrange("p (t c) -> p t c", t=NT), ACT.Copy), sem("fox_v"))
            act.wait_ge(sem("forget_abs"), 1)
            done(act.activation(fg[2], fg[1], ACT.Exp, scale=-1.0), sem("forget_exp"))
            act.wait_ge(sem("forget_1p"), 1)
            done(act.activation(fg[3], fg[2], ACT.Ln), sem("forget_ln"))
            act_attention(done, "fox", fox_batches)
            act_copy_turned(done, uT, "fox_o")
            act_moe(done, 0)
            act_row_norms(done, "mix1", (layer_added, NT))
            act_copy_turned(done, uT, "kv")
            def key_norm_and_values(i):
                c = 2 + 2 * i
                act_head_squares(done, "kvn", i, U_KV + c, c % 4, squares_kv)
                act.wait_ge(unit_done, U_KV + c + 2)
                done(act.activation(v_b[:, i], PS[:, (c + 1) % 4, :].rearrange("p (t c) -> p t c", t=NT), ACT.Copy),
                     sem("kv_values"))

            for i in range(4):
                if i in (0, 2):
                    key_norm_and_values(i // 2)
                act.wait_ge(sem("kv_turned2"), i + 1)
                src = PS[:, 4:6, :].rearrange("p b (g t) -> p (b g) t", g=2)
                for par in range(2):
                    rows = slice(par * DH, (par + 1) * DH)
                    if i < 2:
                        for g in range(G):
                            v = src[rows, g].rearrange("p (n m a) -> p a n m", n=NB, a=2)[:, par]
                            o = flat[i][rows, :, g * NB:(g + 1) * NB].rearrange("p m n -> p n m")
                            done(act.activation(o, v, ACT.Copy), sem("kv_copied"))
                    else:
                        done(act.activation(kz_b[rows, i - 2, :, par, :], src[rows], ACT.Copy), sem("kv_copied"))
            for c in range(2):
                act.wait_ge(unit_done, U_CMP + 4 * c + 4)
                if c == 1:
                    act.wait_ge(sem("cmp_k"), 1)
                for i in range(2):
                    done(act.activation(hidden[:, i, :], PS[:, 4 + i, 0:G * NB], ACT.Silu), sem("cmp_hidden"))
                if c == 0:
                    act.wait_ge(sem("cmp_k"), 1)
                    done(act.activation(kc_rows[0:G * NB, 0, :], PS[0:G * NB, 6, 0:DH], ACT.Square,
                                        accum_out=small[0:G * NB, 72:73]), sem("cmp_k_sq"))
                    act.wait_ge(sem("cmp_k_mean"), 1)
                    done(act.activation(small[0:G * NB, 74:75], small[0:G * NB, 73:74], ACT.Sqrt), sem("cmp_k_root"))
            act_copy_turned(done, uT, "mix1")
            act.wait_ge(sem("gates_biased"), 1)
            done(act.activation(gates[:, :, :], gates[:, :, :], ACT.Sigmoid), sem("gates_ready"))
            for j in range(4):
                act_head_squares(done, "qn", j, U_Q + j, j)
            act_copy_turned(done, qT, "q")
            act.wait_ge(sem("cmp_shifted"), NT)
            done(act.activation(cmp_buf, cmp_buf, ACT.Exp), sem("cmp_exp"))
            act.wait_ge(sem("cmp_probs_turned"), 1)
            done(act.activation(cmp_T[0:H * NB, :], PS[0:H * NB, 7, 0:SEQ], ACT.Copy), sem("cmp_probsT"))
            act_copy_turned(done, qT, "q_rotated")
            act_attention(done, "nsa", nsa_batches)
            act_copy_turned(done, uT, "nsa_o")
            act_moe(done, 1)

        @block.vector
        def _(dve):
            done = Steps(dve, dve_step)
            dve.wait_ge(consts, 1)
            dve.wait_ge(params, 16 * N_PARAMS)
            TWO_PI = 2 * np.pi
            c1 = 6.28125
            c2 = float(np.float32(np.float16(TWO_PI - c1)))
            c3 = float(TWO_PI - c1 - c2)
            BIG = 1.5 * 2.0 ** 23
            pos_f, turns, tmp = small[:, 0:2], small[:, 2:18], small[:, 18:34]
            ang = sin_t[:, :, :].rearrange("p t r -> p (t r)")
            cosv = cos_t[:, :, :].rearrange("p t r -> p (t r)")
            done(dve.tensor_copy(pos_f, pos_i[:, :]))
            for t in range(NT):
                done(dve.tensor_scalar(sin_t[:, t, :], freq[:, :], pos_f[:, t:t + 1], None, ALU.mult))
            done(dve.tensor_scalar(turns, ang, 1.0 / TWO_PI, None, ALU.mult))
            done(dve.tensor_scalar(turns, turns, BIG, None, ALU.add))
            done(dve.tensor_scalar(turns, turns, -BIG, None, ALU.add))
            for c in (c1, c2, c3):
                done(dve.scalar_tensor_tensor(out=ang, in0=turns, scalar=-c, in1=ang, op0=ALU.mult, op1=ALU.add))

            def fold(x, last=None):
                done(dve.tensor_scalar(tmp, x, float(np.pi), -TWO_PI, ALU.is_gt, ALU.mult))
                done(dve.tensor_tensor(x, x, tmp, ALU.add))
                done(dve.tensor_scalar(x, x, 3.1415925, -3.1415925, ALU.min, ALU.max), last)

            done(dve.tensor_scalar(cosv, ang, float(np.pi / 2), None, ALU.add))
            fold(cosv, sem("angles"))
            fold(ang, sem("angles"))
            done(dve.tensor_scalar(gain_qa[:, :], gain_qa[:, :], QK_SCALE, None, ALU.mult))
            done(dve.tensor_scalar(gain_qb[:, :], gain_qb[:, :], QK_SCALE, None, ALU.mult))
            dve.wait_ge(cond_ready, 1)

            def signal_cond():
                dve.tensor_copy(cond_cols, cond[:, :].unsqueeze(2).to_broadcast([P, KC, P])).then_inc(cond_ready, 1)

            signal_cond()
            dve.wait_ge(cond_ready, 2)
            dve.wait_ge(x_loaded, 16 * NT)
            dve_row_norms(done, "mix0")
            done(dve.memset(kz_a, 0.0), sem("kz_zeroed"))
            dve_ada(done, U_ADA[0], 24, ada, (bias_loaded, 16))
            dve_modulate(done, ada[:, SH_M, :], ada[:, SC_M, :], 0, False, rows_modulated)
            done(dve.tensor_copy(head_row, ident[:, 0:H].unsqueeze(2).to_broadcast([P, H, P])))
            for j in range(8):
                if j >= 2:
                    dve.wait_ge(sem("fox_turned"), j - 1)
                dve_head_norm(done, "foxn", j, j % 4,
                              normed[j % 2].rearrange("p (t h d) -> p t h d", t=NT, h=4),
                              (gain_qa if j < 4 else gain_ka)[:, :], sem("fox_normed"))
            dve.wait_ge(sem("forget_out"), 1)
            z, az, ez, lnz, logf = fg
            done(dve.tensor_tensor(z.rearrange("p (t h) -> p t h", t=NT),
                                   PS[:, 6, 0:2 * H].rearrange("p (t h) -> p t h", t=NT),
                                   bias_f[:, :].unsqueeze(1).to_broadcast([P, NT, H]), ALU.add))
            done(dve.tensor_scalar(az, z, -1.0, None, ALU.mult))
            done(dve.tensor_tensor(az, az, z, ALU.max), sem("forget_abs"))
            done(dve.memset(cum, 0.0))
            dve.wait_ge(sem("forget_exp"), 1)
            done(dve.tensor_scalar(ez, ez, 1.0, None, ALU.add), sem("forget_1p"))
            done(dve.tensor_scalar(z, z, 0.0, None, ALU.min))
            dve.wait_ge(sem("forget_ln"), 1)
            done(dve.tensor_tensor(logf, z, lnz, ALU.subtract), sem("logf_ready"))
            dve.wait_ge(sem("cum_out"), 1)
            done(dve.tensor_copy(cum[:, :, 0:H], PS[:, 7, 0:2 * H].rearrange("p (t h) -> p t h", t=NT)),
                 sem("cum_ready"))
            dve.wait_ge(sem("cum_turned"), 1)
            done(dve.tensor_copy(cumT, PS[:, 6, 0:SEQ]))
            done(dve.tensor_scalar(ncumT, cumT, -1.0, None, ALU.mult), sem("cumT_ready"))

            def fox_finish(b, heads, rinv):
                br, t, g = fox_batches[b]
                dve.wait_ge(heads_out, b + 1)
                done(dve.tensor_tensor(u[:, t, g * UC:(g + 1) * UC].rearrange("p (i d) -> p i d", i=4), heads,
                                       rinv.unsqueeze(2).to_broadcast([P, 4, DH]), ALU.mult), heads_read)

            dve_attention(done, "fox", fox_batches, fox_finish)

            def add_mix(layer, u0):
                for j in range(4):
                    dve.wait_ge(unit_done, u0 + j + 1)
                    cols = slice(j * UC, (j + 1) * UC)
                    dve_add_rows(done, cols, PS[:, 4 + j, :].rearrange("p (t c) -> p t c", t=NT),
                                 ada[:, G_M, cols], mix_added)

            add_mix(0, U_OUT_A)
            dve_moe(done, 0)

            signal_cond()
            dve.wait_ge(cond_ready, 3)
            dve_row_norms(done, "mix1")
            dve_ada(done, U_ADA[1], 24, ada, (bias_loaded, 32))
            dve_ada(done, U_ADA_KV, 8, ada_kv, (bias_kv_loaded, 16))
            dve_modulate(done, ada_kv[:, 0, :], ada_kv[:, 1, :], 2, False, rows_modulated)
            done(dve.memset(kz_b, 0.0))
            done(dve.memset(small[:, 0:32], 0.0))
            for j in range(2):
                dve.wait_ge(unit_done, U_KV + j + 1)
                for t in range(NT):
                    for c in range(2):
                        done(dve.tensor_tensor(doubled[j][:, t, :, c, :],
                                               PS[:, j, t * UC:(t + 1) * UC].rearrange("p (g d) -> p g d", g=G),
                                               pe[:, j, :].unsqueeze(1).to_broadcast([P, G, DH]), ALU.add),
                             sem("kv_doubled") if t == 1 and c == 1 else None)
            for i, j in enumerate((2, 4)):
                dve.wait_ge(sem("kv_turned2"), i + 1)
                dve_head_norm(done, "kvn", i, j % 4, new_keys, gain_kb[:, 1 + i, :], None, squares_kv)
                dve_rope(done, new_keys, G, rope_tmp_k, None)
                for t in range(NT):
                    for c in range(2):
                        done(dve.tensor_copy(doubled[i][:, t, :, c, :], new_keys[:, t]),
                             sem("kv_doubled") if (t == 1 and c == 1) else None)
            dve.wait_ge(sem("cmp_k_sq"), 1)
            R16 = slice(0, G * NB)
            done(dve.tensor_scalar(small[R16, 73:74], small[R16, 72:73], 1.0 / DH, EPS, ALU.mult, ALU.add),
                 sem("cmp_k_mean"))
            dve.wait_ge(sem("cmp_k_root"), 1)
            done(dve.reciprocal(small[R16, 75:76], small[R16, 74:75]))
            for c in range(2):
                done(dve.scalar_tensor_tensor(out=kc_rows[R16, c, :], in0=PS[R16, 6, 0:DH],
                                              scalar=small[R16, 75:76], in1=gain_kb[R16, 0, :],
                                              op0=ALU.mult, op1=ALU.mult), sem("cmp_k_normed") if c else None)
            dve.wait_ge(sem("cmp_k_turned"), 1)
            for par in range(2):
                rows = slice(par * DH, (par + 1) * DH)
                done(dve.tensor_copy(kcz[rows, par, :], PS[rows, 6, 0:G * NB]), sem("kcz_ready"))
            dve.wait_ge(sem("cmp_hidden"), 4)
            for i in range(2):
                done(dve.tensor_copy(hidden_rep[:, i, :].rearrange("p (g i n) -> p g i n", g=G, i=HPG),
                                     hidden[:, i, :].rearrange("p (g n) -> p g n", g=G).unsqueeze(2)
                                     .to_broadcast([P, G, HPG, NB])), sem("cmp_rep"))
            dve.wait_ge(sem("cmp_v"), 1)
            RV = slice(0, H * NB)
            done(dve.tensor_copy(v_cmp_rows[RV, :], PS[RV, 7, 0:DH]))
            done(dve.tensor_tensor(v_diag[RV], v_cmp_rows[RV, :].unsqueeze(1).to_broadcast([H * NB, H, DH]),
                                   block_diag[:, :].unsqueeze(2).to_broadcast([H * NB, H, DH]), ALU.mult))
            dve_modulate(done, ada[:, SH_M, :], ada[:, SC_M, :], 3, False, rows_modulated, mod_tmp_q)
            dve.wait_ge(sem("gates_out"), 1)
            done(dve.tensor_tensor(gates[:, :, :], PS[:, 6, 0:NT * 3 * H].rearrange("p (t c) -> p t c", t=NT),
                                   bias_gate[:, :].unsqueeze(1).to_broadcast([P, NT, 3 * H]), ALU.add),
                 sem("gates_biased"))
            for j in range(4):
                dve_head_norm(done, "qn", j, j,
                              q_rows[:, :, j * UC:(j + 1) * UC].rearrange("p t (h d) -> p t h d", h=4),
                              gain_qb[:, :], sem("q_normed"))
            for t in range(NT):
                for n in range(NB):
                    first = (n + 1) * CMP - 1 - t * P
                    if first <= 0:
                        done(dve.memset(visible[:, t, n:n + 1], 1.0))
                    elif first >= P:
                        done(dve.memset(visible[:, t, n:n + 1], 0.0))
                    else:
                        done(dve.tensor_scalar(visible[:, t, n:n + 1], partition_no[:, :], float(first),
                                               None, ALU.is_ge))
            done(dve.tensor_scalar(hidden_mask, visible, -1.0, -MASKED, ALU.add, ALU.mult))
            dve.wait_ge(sem("cmp_logits"), 1)
            for t in range(NT):
                x = cmp_buf[:, t, :].rearrange("p (h n) -> p h n", h=H)
                src = PS[:, 6, t * H * NB:(t + 1) * H * NB].rearrange("p (h n) -> p h n", h=H)
                done(dve.tensor_tensor(x, src, visible[:, t, :].unsqueeze(1).to_broadcast([P, H, NB]), ALU.mult))
                done(dve.tensor_tensor(x, x, hidden_mask[:, t, :].unsqueeze(1).to_broadcast([P, H, NB]), ALU.add))
                done(dve.tensor_reduce(small[:, 32:48], x, AX.X, ALU.max))
                done(dve.tensor_tensor(x, x, small[:, 32:48].unsqueeze(2).to_broadcast([P, H, NB]), ALU.subtract),
                     sem("cmp_shifted"))
            dve.wait_ge(sem("cmp_exp"), 1)
            for t in range(NT):
                x = cmp_buf[:, t, :].rearrange("p (h n) -> p h n", h=H)
                done(dve.tensor_reduce(small[:, 32:48], x, AX.X, ALU.add))
                done(dve.reciprocal(small[:, 32:48], small[:, 32:48]))
                done(dve.tensor_tensor(x, x, visible[:, t, :].unsqueeze(1).to_broadcast([P, H, NB]), ALU.mult))
                done(dve.tensor_tensor(x, x, small[:, 32:48].unsqueeze(2).to_broadcast([P, H, NB]), ALU.mult),
                     sem("cmp_probs"))

            def gate_of(t, h0, n, br):
                return gates[:, t, :].rearrange("p (h b) -> p b h", b=3)[:, br, h0:h0 + n]

            dve.wait_ge(rows_turned, 4 * TURNED.index("q") + 4)
            dve_rope(done, q_rows.rearrange("p t (h d) -> p t h d", h=H), H, rope_tmp_q, sem("q_rotated"))
            for t in range(NT):
                dve.wait_ge(sem("cmp_heads"), 2 * t + 2)
                done(dve.tensor_tensor(u[:, t, :].rearrange("p (h d) -> p h d", h=H),
                                       PS[:, 2 * t:2 * t + 2, :].rearrange("p b (h d) -> p (b h) d", h=8),
                                       gate_of(t, 0, H, 0).unsqueeze(2).to_broadcast([P, H, DH]), ALU.mult),
                     sem("cmp_heads_read"))

            def nsa_finish(b, heads, rinv):
                br, t, g = nsa_batches[b]
                dve.wait_ge(heads_out, BATCHES_FROM["nsa"] + b + 1)
                done(dve.tensor_tensor(rinv, rinv, gate_of(t, 4 * g, 4, 1 + br), ALU.mult))
                done(dve.tensor_tensor(head_tmp, heads, rinv.unsqueeze(2).to_broadcast([P, 4, DH]), ALU.mult),
                     heads_read)
                o = u[:, t, g * UC:(g + 1) * UC].rearrange("p (i d) -> p i d", i=4)
                done(dve.tensor_tensor(o, o, head_tmp, ALU.add), sem("nsa_o"))

            dve_attention(done, "nsa", nsa_batches, nsa_finish)
            add_mix(1, U_OUT_B)
            dve_moe(done, 1)


_INS = ["x", "c", "positions", "w_ada", "b_ada", "norm_mix", "norm_ffn", "w_in_a", "b_f_a", "qnorm_a", "knorm_a",
        "w_o_a", "norm_kv", "w_ada_kv", "b_ada_kv", "w_kv_b", "pe_cmp_k", "pe_cmp_v", "w_cmp_k1", "w_cmp_k2",
        "w_cmp_v1", "w_cmp_v2", "knorm_b", "w_in_b", "b_gate_b", "qnorm_b", "w_o_b", "w_router", "b_router",
        "w_exp_gate", "w_exp_up", "w_exp_down", "w_sh_gate", "w_sh_up", "w_sh_down"]


def kernel(**inputs):
    import numpy as _np
    import concourse.bacc as _bacc
    from concourse import mybir as _mybir
    from concourse.bass_utils import run_bass_kernel_spmd as _run

    nc = _bacc.Bacc("TRN2", target_bir_lowering=False, num_devices=1)
    arrays, args = {}, {}
    for name in _INS:
        x = _np.ascontiguousarray(inputs[name])
        arrays[f"in_{name}"] = x
        args[name] = nc.dram_tensor(f"in_{name}", x.shape, _mybir.dt.from_np(x.dtype), kind="ExternalInput").ap()
    out = nc.dram_tensor("out_0", (1, SEQ, D), _mybir.dt.float32, kind="ExternalOutput").ap()
    build(nc, args, out)
    r = _run(nc, [arrays], core_ids=[0])
    return r.results[0]["out_0"]
```

```python
from contextlib import ExitStack

import numpy as np

import concourse.bass as bass
from concourse import mybir

F32 = mybir.dt.float32
I32 = mybir.dt.int32
ALU = mybir.AluOpType
ACT = mybir.ActivationFunctionType
AX = mybir.AxisListType

P = 128
D = 1024
SEQ = 256
NT = SEQ // P
KC = D // P
DH = 64
H = 16
G = 4
HPG = H // G
ROPE_HALF = DH // 8
ROPE_THETA = 500000.0
CMP = 64
NB = SEQ // CMP
N_EXP = 64
D_EXP = 256
EPS = 1e-6
MASKED = -1e30
ROUTED_SCALE = 2.5
QK_SCALE = DH ** -0.5

UC = 256
UNIT = KC * UC
SLOTS = 12
BODY = SLOTS // 3
TURNS = N_EXP // BODY
PASS = 64
MAX_PASSES = SEQ // PASS
TABLE = N_EXP + 4

U_ADA = [0, 0]
U_QKV = U_ADA[0] + 6 * D // UC
U_OUT_A = U_QKV + 3 * D // UC
U_SHARED = [U_OUT_A + D // UC, 0]
U_EXPERTS = [U_SHARED[0] + 3, 0]
U_ADA[1] = U_EXPERTS[0] + 3 * N_EXP
U_ADA_KV = U_ADA[1] + 6 * D // UC
U_KV = U_ADA_KV + 2 * D // UC
U_CMP = U_KV + 6 * G * DH // UC
U_Q = U_CMP + 2 * 4
U_OUT_B = U_Q + D // UC
U_SHARED[1] = U_OUT_B + D // UC
U_EXPERTS[1] = U_SHARED[1] + 3
U_END = U_EXPERTS[1] + 3 * N_EXP

SH_M, SC_M, G_M, SH_F, SC_F, G_F = range(6)


class Steps:

    def __init__(self, eng, step):
        self.eng, self.step, self.count = eng, step, {}

    def __call__(self, ins, sem=None):
        sem = sem or self.step
        ins.then_inc(sem, 1)
        self.count[sem.name] = self.count.get(sem.name, 0) + 1
        self.eng.wait_ge(sem, self.count[sem.name])


def attention_batches(kind):
    branches = (0,) if kind == "fox" else (0, 1)
    return [(br, t, g) for br in branches for t in range(NT) for g in range(H // 4)]


def build(nc, a, out):
    with ExitStack() as ctx:
        def sb(name, shape, dt=F32):
            return ctx.enter_context(nc.sbuf_tensor(name, shape, dt))

        sems = {}

        def sem(name):
            if name not in sems:
                sems[name] = ctx.enter_context(nc.semaphore(name))
            return sems[name]

        PS = ctx.enter_context(nc.psum_tensor("PS", [P, 8, 512], F32))
        ring = sb("ring", [P, SLOTS, UNIT])
        h = sb("h", [P, NT, D])
        u = sb("u", [P, NT, D])
        uT = sb("uT", [P, KC, SEQ])
        ada = sb("ada", [P, 6, D])
        gain = sb("gain", [P, D])
        scratch = sb("scratch", [P, 12288])
        ident = sb("ident", [P, P])
        ones = sb("ones", [P, P])
        upto = sb("upto", [P, P])
        before = sb("before", [P, P])
        causal = sb("causal", [P, 2 * P])
        iota = sb("iota", [P, SEQ])
        block_diag = sb("block_diag", [H * NB, H])
        cond = sb("cond", [P, KC])
        pos_i = sb("pos_i", [P, NT], I32)
        freq = sb("freq", [P, ROPE_HALF])
        cos_t = sb("cos_t", [P, NT, ROPE_HALF])
        sin_t = sb("sin_t", [P, NT, ROPE_HALF])
        gain_qa = sb("gain_qa", [P, DH])
        gain_ka = sb("gain_ka", [P, DH])
        gain_qb = sb("gain_qb", [P, DH])
        gain_kb = sb("gain_kb", [P, 3, DH])
        bias_f = sb("bias_f", [P, H])
        bias_gate = sb("bias_gate", [P, 3 * H])
        bias_router = sb("bias_router", [P, 2, N_EXP])
        pe = sb("pe", [P, 2, DH])
        w_gates = sb("w_gates", [P, KC, 3 * H])
        w_forget = w_gates[:, :, 0:H]
        partition_no = sb("partition_no", [P, 1])
        gates = sb("gates", [P, NT, 3 * H])
        small = sb("small", [P, 96])
        stats = sb("stats", [P, 3, 16])
        slot_of = sb("slot_of", [P, NT, TABLE])
        weight_of = sb("weight_of", [P, NT, TABLE])
        passes_i = sb("passes_i", [1, 2, TABLE], I32)

        def cut(at, shape):
            n = int(np.prod(shape))
            v = scratch[:, at:at + n]
            names = " ".join(f"d{i}" for i in range(len(shape)))
            return v if len(shape) == 1 else v.rearrange(f"p ({names}) -> p {names}", **{
                f"d{i}": s for i, s in enumerate(shape)})

        qT = cut(0, [KC, SEQ])
        kz_a = cut(2048, [H, SEQ])
        v_a = cut(6144, [NT, D])
        q_rows = cut(2048, [NT, D])
        kz_b = cut(4096, [2, G, 2, SEQ])
        v_b = cut(8192, [2, NT, G * DH])
        S0 = 9216
        softmax_in = [cut(S0, [4 * SEQ]), cut(S0 + 1024, [4 * SEQ])]
        pT = cut(S0 + 2048, [4 * SEQ])
        squares = cut(S0, [512])
        normed = [cut(S0 + 1024, [512]), cut(S0 + 1536, [512])]
        cond_cols = cut(S0 + 2048, [KC, P])
        scaled = [cut(6144, [UC]), cut(6144 + UC, [UC])]
        ada_kv = cut(0, [2, D])
        doubled = [cut(S0, [NT, G, 2, DH]), cut(S0 + 1024, [NT, G, 2, DH])]
        flat = [cut(2048, [32, G * NB]), cut(2560, [32, G * NB])]
        hidden = cut(3072, [2, G * NB])
        hidden_rep = cut(3104, [2, H * NB])
        kc_rows = cut(3232, [2, DH])
        w_cmp2 = cut(3360, [2, 2, DH])
        kcz = small[:, 0:2 * G * NB].rearrange("p (a b) -> p a b", a=2)
        new_keys = cut(0, [NT, G, DH])
        rope_tmp_k = cut(512, [4 * G * ROPE_HALF])
        v_cmp_rows = cut(640, [DH])
        squares_kv = cut(1024, [512])
        v_diag = cut(S0 + 2048, [H, DH])
        cmp_buf = cut(S0, [NT, H * NB])
        cmp_T = cut(S0 + 256, [SEQ])
        visible = cut(S0 + 512, [NT, NB])
        hidden_mask = cut(S0 + 528, [NT, NB])
        uT_flat = uT[:, :, :].rearrange("p k t -> p (k t)")
        cum = uT_flat[:, 0:2 * P].rearrange("p (t c) -> p t c", t=NT)
        cumT = uT_flat[:, 256:512]
        ncumT = uT_flat[:, 512:768]
        fg = [uT_flat[:, 768 + 32 * i:800 + 32 * i] for i in range(5)]
        head_row = ada[:, 0:2, :].rearrange("p a d -> p (a d)").rearrange("p (h m) -> p h m", h=H)
        x_pair = [cut(0, [KC, 2 * PASS]), cut(1024, [KC, 2 * PASS])]
        one_hot = [cut(2048, [NT, 2 * PASS]), cut(2304, [NT, 2 * PASS])]
        hot_w = cut(2560, [NT, 2 * PASS])
        turned_sb = cut(2816, [512])
        hidT, hot_wT = turned_sb[:, 0:256].rearrange("p (j s) -> p j s", j=2), turned_sb[:, 256:512]
        gate_act = cut(3328, [D_EXP])
        h_rows = cut(3584, [D_EXP])
        y_rows = cut(3840, [D])
        x_more = cut(4864, [KC, PASS])
        hot_more = cut(5376, [NT, PASS])
        sh_act = cut(5504, [2, SEQ])
        sh_hid = cut(6016, [2, SEQ])
        scores = cut(6528, [NT, N_EXP])
        chosen_by = cut(6656, [NT, N_EXP])
        replaced = cut(6784, [NT, N_EXP])
        routed = cut(6912, [NT, N_EXP])
        passes_f = cut(7040, [P])
        top8 = cut(7168, [NT, 8])
        rsum = cut(7184, [NT])
        w_router = cut(7200, [KC, N_EXP])
        mod_tmp = cut(8192, [D])
        mod_tmp_q = cut(S0, [D])
        rope_tmp_q = cut(S0 + 1024, [4 * H * ROPE_HALF])
        head_tmp = cut(2048, [4, DH])
        g_tmp = cut(8192, [D])

        slot_loaded = [sem(f"slot_loaded{i}") for i in range(SLOTS)]
        unit_done = sem("unit_done")
        params = sem("params_loaded")
        x_loaded = sem("x_loaded")
        gain_loaded = sem("gain_loaded")
        gain_used = sem("gain_used")
        bias_loaded = sem("ada_bias_loaded")
        late_biases_loaded = sem("late_biases_loaded")
        consts = sem("consts_ready")
        ones_ready = sem("ones_ready")
        pool_step = sem("pool_step")
        dve_step = sem("dve_step")
        act_step = sem("act_step")
        cond_loaded = sem("cond_loaded")
        cond_ready = sem("cond_ready")
        layer_added = sem("layer_added")
        router_loaded = sem("router_loaded")
        nsa_params = sem("nsa_params_loaded")
        stored = sem("stored")
        TURNED = ["mix0", "fox_o", "ffn0", "kv", "mix1", "q", "q_rotated", "nsa_o", "ffn1"]
        MODULATED = ["mix0", "ffn0", "kv", "mix1", "ffn1"]
        NORMED = ["mix0", "ffn0", "mix1", "ffn1"]
        HEADS_FROM = {"foxn": 0, "kvn": 8, "qn": 10}
        BATCHES_FROM = {"fox": 0, "nsa": 8}
        rows_turned, rows_copied, rows_modulated = sem("rows_turned"), sem("rows_copied"), sem("rows_modulated")
        row_squares, row_means, row_roots = sem("row_squares"), sem("row_means"), sem("row_roots")
        head_squares, head_means, head_roots = sem("head_squares"), sem("head_means"), sem("head_roots")
        logits_out, scores_read, scores_shifted = sem("logits_out"), sem("scores_read"), sem("scores_shifted")
        probs_ready, probs_turned, probsT_ready = sem("probs_ready"), sem("probs_turned"), sem("probsT_ready")
        heads_out, heads_read = sem("heads_out"), sem("heads_read")
        ada_scaled = sem("ada_scaled")
        ada_read = sem("ada_read")
        mix_added = sem("mix_added")

        def landed(eng, n):
            eng.wait_ge(slot_loaded[n % SLOTS], 16 * (n // SLOTS + 1))

        def slot(n, k=KC):
            return ring[:, n % SLOTS, :].rearrange("p (k c) -> p k c", k=k)

        def bcast(ap, shape):
            return ap.to_broadcast(shape)

        MOE_SEMS = ["router_out", "scores_ready", "mask_ready", "ranks_out", "passes_ready", "passes_out",
                    "tables_ready", "shared_act", "shared_hid", "onehot_ready", "gathered", "x_ready",
                    "gu_out", "gate_ready", "hid_ready", "hot_w_ready", "turned", "turned_copied",
                    "y_out", "y_ready",
                    "more_onehot", "more_gathered", "more_x", "more_gu", "more_gate", "more_hid",
                    "more_turned", "more_copied", "more_y_out", "more_y", "more_added"]
        moe_sem = [{n: sem(f"{n}{layer}") for n in MOE_SEMS} for layer in range(2)]

        def pe_turn_rows(pe_, src, ready, what, banks_free=()):
            pe_.wait_ge(*ready)
            for s, n in banks_free:
                pe_.wait_ge(s, n)
            for b in range(KC // 2):
                for k in (2 * b, 2 * b + 1):
                    for t in range(NT):
                        mm = pe_.transpose(PS[:, b, (k % 2) * SEQ + t * P:(k % 2) * SEQ + (t + 1) * P],
                                           src[:, t, k * P:(k + 1) * P], ident[:, :])
                mm.then_inc(rows_turned, 1)
            pe_.wait_ge(rows_copied, 4 * TURNED.index(what) + 4)

        def act_copy_turned(done, dst, what):
            for b in range(KC // 2):
                done.eng.wait_ge(rows_turned, 4 * TURNED.index(what) + b + 1)
                done(done.eng.activation(dst[:, 2 * b:2 * b + 2, :].rearrange("p k t -> p (k t)"),
                                         PS[:, b, :], ACT.Copy), rows_copied)

        def pe_rows_unit(pe_, n, bank, lhs):
            landed(pe_, n)
            w = slot(n)
            for t in range(NT):
                for k in range(KC):
                    mm = pe_.matmul(PS[:, bank, t * UC:(t + 1) * UC], lhs[:, k, t * P:(t + 1) * P],
                                    w[:, k, :], start=(k == 0), stop=(k == KC - 1))
            mm.then_inc(unit_done, 1)

        ADA_BANKS = 8
        ADA_FIRST = 12

        def ada_pieces(layer):
            bufs = [(U_ADA[layer], ada, 6)] + ([(U_ADA_KV, ada_kv, 2)] if layer else [])
            return [(u0 + j, buf[:, j // 4, (j % 4) * UC:(j % 4 + 1) * UC])
                    for u0, buf, n in bufs for j in range(n * D // UC)]

        ADA_ALONE = [0, 4]

        def ada_bank(layer, j):
            return (j + ADA_ALONE[layer]) % ADA_BANKS

        def on_vector(layer):
            return [j for j in range(len(ada_pieces(layer))) if j % 2 and j >= ADA_ALONE[layer]]

        def ada_read_before(layer):
            return len(ada_pieces(0)) * layer

        def pe_ada(pe_, layer):
            vec0 = len(on_vector(0)) * layer
            pe_.wait_ge(bias_loaded, 16 if layer == 0 else 32)
            for j, (n, dst) in enumerate(ada_pieces(layer)):
                o = PS[:, ada_bank(layer, j), 0:UC]
                if layer == 1:
                    if j == ADA_ALONE[1]:
                        pe_.wait_ge(layer_added, NT)
                    if j == G_F * D // UC:
                        pe_.wait_ge(late_biases_loaded, 16 * 2)
                if j >= ADA_BANKS:
                    pe_.wait_ge(ada_read, ada_read_before(layer) + j - ADA_BANKS + 1)
                pe_.matmul(o, ones[0:1, :], dst[0:1], start=True, stop=False)
                if j in on_vector(layer):
                    v = on_vector(layer).index(j)
                    pe_.wait_ge(ada_scaled, vec0 + v + 1)
                    mm = pe_.matmul(o, ones[:, :], scaled[v % 2], start=False, stop=True)
                else:
                    landed(pe_, n)
                    for k in range(KC):
                        mm = pe_.matmul(o, cond_cols[:, k, :], slot(n)[:, k, :], start=False, stop=(k == KC - 1))
                mm.then_inc(unit_done, 1)
            pe_.wait_ge(ada_read, ada_read_before(layer) + len(ada_pieces(layer)))

        def act_ada(done, layer, first, last):
            for j, (n, dst) in list(enumerate(ada_pieces(layer)))[first:last]:
                done.eng.wait_ge(unit_done, n + 1)
                done(done.eng.activation(dst, PS[:, ada_bank(layer, j), 0:UC], ACT.Copy), ada_read)

        def dve_ada(done, layer, first, last):
            eng, pieces, mine = done.eng, ada_pieces(layer), on_vector(layer)
            for v, j in enumerate(mine):
                if not first <= j < last:
                    continue
                n, acc = pieces[j][0], scaled[v % 2]
                if v >= 2:
                    eng.wait_ge(unit_done, pieces[mine[v - 2]][0] + 1)
                landed(eng, n)
                done(eng.tensor_scalar(acc, slot(n)[:, 0, :], cond[:, 0:1], None, ALU.mult))
                for k in range(1, KC):
                    done(eng.scalar_tensor_tensor(out=acc, in0=slot(n)[:, k, :], scalar=cond[:, k:k + 1], in1=acc,
                                                  op0=ALU.mult, op1=ALU.add), ada_scaled if k == KC - 1 else None)

        def width(t):
            return (t + 1) * P

        def logit_banks(b):
            return PS[:, 2 * (b % 2):2 * (b % 2) + 2, :].rearrange("p b (i w) -> p (b i) w", i=2)

        def pe_attention(pe_, kind, batches, keys, values):
            b0 = BATCHES_FROM[kind]

            def logits(b):
                br, t, g = batches[b]
                w = width(t)
                if b >= 2:
                    pe_.wait_ge(scores_read, b0 + b - 1)
                o = logit_banks(b)
                for i in range(4):
                    hd = 4 * g + i
                    mm = pe_.matmul(o[:, i, 0:w], qT[:, hd // 2, t * P:(t + 1) * P], keys(br, hd)[:, 0:w],
                                    start=True, stop=(kind != "fox"))
                    if kind == "fox":
                        pe_.matmul(o[:, i, 0:w].rearrange("p (c m) -> p c m", m=P),
                                   cumT[:, t * P:(t + 1) * P],
                                   head_row[:, hd:hd + 1, :].to_broadcast([P, w // P, P]),
                                   start=False, stop=False)
                        mm = pe_.matmul(o[:, i, 0:w], head_row[:, hd, :], ncumT[:, 0:w], start=False, stop=True)
                mm.then_inc(logits_out, 1)

            def turn(b):
                br, t, g = batches[b]
                w = width(t)
                pe_.wait_ge(probs_ready, 4 * (b0 + b + 1))
                if b >= 1:
                    pe_.wait_ge(probsT_ready, b0 + b)
                p = softmax_in[b % 2]
                for n in range(4 * (t + 1)):
                    mm = pe_.transpose(PS[:, 4 + n // 4, (n % 4) * P:(n % 4 + 1) * P],
                                       p[:, n * P:(n + 1) * P], ident[:, :])
                mm.then_inc(probs_turned, 1)

            def weigh(b):
                br, t, g = batches[b]
                pe_.wait_ge(probsT_ready, b0 + b + 1)
                if b >= 2:
                    pe_.wait_ge(heads_read, b0 + b - 1)
                for i in range(4):
                    for kt in range(t + 1):
                        n = i * (t + 1) + kt
                        mm = pe_.matmul(PS[:, 6 + b % 2, i * DH:(i + 1) * DH], pT[:, n * P:(n + 1) * P],
                                        values(br, kt, 4 * g + i), start=(kt == 0), stop=(kt == t))
                mm.then_inc(heads_out, 1)

            logits(0)
            for b in range(len(batches)):
                if b + 1 < len(batches):
                    logits(b + 1)
                if b >= 1:
                    weigh(b - 1)
                turn(b)
            weigh(len(batches) - 1)

        def act_attention(done, kind, batches):
            eng, b0 = done.eng, BATCHES_FROM[kind]

            def copy(b):
                n = 4 * width(batches[b][1])
                eng.wait_ge(probs_turned, b0 + b + 1)
                if b >= 1:
                    eng.wait_ge(heads_out, b0 + b)
                done(eng.activation(pT[:, 0:n], PS[:, 4:4 + n // 512, :].rearrange("p b c -> p (b c)"), ACT.Copy),
                     probsT_ready)

            for b, (br, t, g) in enumerate(batches):
                w = width(t)
                eng.wait_ge(scores_shifted, b0 + b + 1)
                for i in range(4):
                    p = softmax_in[b % 2][:, i * w:(i + 1) * w]
                    done(eng.activation(p, p, ACT.Exp, bias=stats[:, b % 3, 4 + i:5 + i],
                                        accum_out=stats[:, b % 3, 8 + i:9 + i]), probs_ready)
                if b >= 1:
                    copy(b - 1)
            copy(len(batches) - 1)

        def dve_attention(done, kind, batches, finish):
            eng, b0 = done.eng, BATCHES_FROM[kind]

            def mask(b):
                br, t, g = batches[b]
                w = width(t)
                eng.wait_ge(logits_out, b0 + b + 1)
                if b >= 2:
                    eng.wait_ge(probs_turned, b0 + b - 1)
                s = softmax_in[b % 2][:, 0:4 * w].rearrange("p (i w) -> p i w", i=4)
                done(eng.tensor_tensor(s, logit_banks(b)[:, :, 0:w],
                                       causal[:, 2 * P - w:2 * P].unsqueeze(1).to_broadcast([P, 4, w]), ALU.add),
                     scores_read)
                done(eng.tensor_reduce(stats[:, b % 3, 0:4], s, AX.X, ALU.max))
                done(eng.tensor_scalar(stats[:, b % 3, 4:8], stats[:, b % 3, 0:4], -1.0, None, ALU.mult),
                     scores_shifted)

            def output(b):
                eng.wait_ge(probs_ready, 4 * (b0 + b + 1))
                done(eng.reciprocal(stats[:, b % 3, 12:16], stats[:, b % 3, 8:12]))
                finish(b, PS[:, 6 + b % 2, 0:4 * DH].rearrange("p (i d) -> p i d", i=4), stats[:, b % 3, 12:16])

            mask(0)
            for b in range(len(batches)):
                if b + 1 < len(batches):
                    mask(b + 1)
                if b >= 1:
                    output(b - 1)
            output(len(batches) - 1)

        def act_row_norms(done, tag, h_ready):
            done.eng.wait_ge(*h_ready)
            for t in range(NT):
                done(done.eng.activation(u[:, t, :], h[:, t, :], ACT.Square, accum_out=small[:, 64 + t:65 + t]),
                     row_squares)
            i = NORMED.index(tag)
            done.eng.wait_ge(row_means, i + 1)
            done(done.eng.activation(small[:, 68:70], small[:, 66:68], ACT.Sqrt), row_roots)

        def dve_row_norms(done, tag):
            eng = done.eng
            i = NORMED.index(tag)
            eng.wait_ge(row_squares, NT * (i + 1))
            done(eng.tensor_scalar(small[:, 66:68], small[:, 64:66], 1.0 / D, EPS, ALU.mult, ALU.add),
                 row_means)
            eng.wait_ge(row_roots, i + 1)
            done(eng.reciprocal(small[:, 70:72], small[:, 68:70]))

        def dve_modulate(done, shift, scale, n_gain, split, ready, mod_tmp=mod_tmp):
            eng = done.eng
            eng.wait_ge(gain_loaded, 16 * (n_gain + 1))
            done(eng.scalar_tensor_tensor(out=scale, in0=scale, scalar=1.0, in1=gain[:, :],
                                          op0=ALU.add, op1=ALU.mult), gain_used)
            for t in range(NT):
                done(eng.scalar_tensor_tensor(out=mod_tmp, in0=h[:, t, :], scalar=small[:, 70 + t:71 + t],
                                              in1=scale, op0=ALU.mult, op1=ALU.mult))
                if split:
                    o = u[:, t, :].rearrange("p (k q) -> p q k", k=KC)
                    i0 = mod_tmp.rearrange("p (q k) -> p q k", k=KC)
                    i1 = shift.rearrange("p (q k) -> p q k", k=KC)
                else:
                    o, i0, i1 = u[:, t, :], mod_tmp, shift
                done(eng.tensor_tensor(o, i0, i1, ALU.add), ready)

        def dve_add_rows(done, cols, banks, gate_row, ready=None):
            eng = done.eng
            n = cols.stop - cols.start
            tmp = g_tmp[:, 0:2 * n].rearrange("p (t c) -> p t c", t=NT)
            done(eng.tensor_tensor(tmp, banks, gate_row.unsqueeze(1).to_broadcast([P, NT, n]), ALU.mult))
            hc = h[:, :, cols]
            done(eng.tensor_tensor(hc, hc, tmp, ALU.add), ready)

        def act_head_squares(done, tag, i, n, bank, squares=squares):
            i += HEADS_FROM[tag]
            done.eng.wait_ge(unit_done, n + 1)
            if i >= 1:
                done.eng.wait_ge(head_means, i)
            done(done.eng.activation(squares, PS[:, bank, :], ACT.Square), head_squares)
            done.eng.wait_ge(head_means, i + 1)
            done(done.eng.activation(small[:, 80:88], small[:, 72:80], ACT.Sqrt), head_roots)

        def dve_head_norm(done, tag, i, bank, dst, gain_row, ready, squares=squares):
            eng = done.eng
            i += HEADS_FROM[tag]
            eng.wait_ge(head_squares, i + 1)
            done(eng.tensor_reduce(small[:, 72:80], squares.rearrange("p (h d) -> p h d", h=8), AX.X, ALU.add))
            done(eng.tensor_scalar(small[:, 72:80], small[:, 72:80], 1.0 / DH, EPS, ALU.mult, ALU.add),
                 head_means)
            eng.wait_ge(head_roots, i + 1)
            done(eng.reciprocal(small[:, 88:96], small[:, 80:88]))
            x = PS[:, bank, :].rearrange("p (h d) -> p h d", h=8)
            for t in range(NT):
                done(eng.tensor_tensor(dst[:, t], x[:, 4 * t:4 * t + 4, :],
                                       small[:, 88 + 4 * t:92 + 4 * t].unsqueeze(2).to_broadcast([P, 4, DH]),
                                       ALU.mult))
            for t in range(NT):
                done(eng.tensor_tensor(dst[:, t], dst[:, t], gain_row.unsqueeze(1).to_broadcast([P, 4, DH]),
                                       ALU.mult), ready if t == NT - 1 else None)

        def dve_rope(done, x, n_heads, tmp, ready):
            eng = done.eng
            n = n_heads * ROPE_HALF
            ta, tb, tc, td = (tmp[:, i * n:(i + 1) * n].rearrange("p (h r) -> p h r", h=n_heads) for i in range(4))
            for t in range(NT):
                x1, x2 = x[:, t, :, 0:ROPE_HALF], x[:, t, :, ROPE_HALF:2 * ROPE_HALF]
                c = cos_t[:, t, :].unsqueeze(1).to_broadcast([P, n_heads, ROPE_HALF])
                s = sin_t[:, t, :].unsqueeze(1).to_broadcast([P, n_heads, ROPE_HALF])
                done(eng.tensor_tensor(ta, x1, c, ALU.mult))
                done(eng.tensor_tensor(tb, x2, s, ALU.mult))
                done(eng.tensor_tensor(tc, x2, c, ALU.mult))
                done(eng.tensor_tensor(td, x1, s, ALU.mult))
                done(eng.tensor_tensor(x1, ta, tb, ALU.subtract))
                done(eng.tensor_tensor(x2, tc, td, ALU.add), ready if t == NT - 1 else None)

        OUT = [PS[:, 0:2, :].rearrange("p b c -> p (b c)"), PS[:, 2:4, :].rearrange("p b c -> p (b c)")]
        GATHER, GU, Y0 = 4, 5, 6

        def pe_gather(pe_, hot, chunks):
            w = 512 // len(chunks)
            for i, k in enumerate(chunks):
                for t in range(NT):
                    mm = pe_.matmul(PS[:, GATHER, i * w:(i + 1) * w], u[:, t, k * P:(k + 1) * P],
                                    hot[:, t, :], start=(t == 0), stop=(t == NT - 1))
            return mm

        def gate_up(n, k):
            s0 = n % SLOTS
            return ring[:, s0:s0 + 2, :].rearrange("p b (k c) -> p b k c", k=KC)[:, :, k, :]

        def pe_gate_up(pe_, units, x):
            for k in range(KC):
                for i, n in enumerate(units):
                    mm = pe_.matmul(PS[i * PASS:(i + 1) * PASS, GU, :].rearrange("p (b c) -> p b c", b=2),
                                    x[:, k, i * PASS:(i + 1) * PASS], gate_up(n, k),
                                    start=(k == 0), stop=(k == KC - 1))
            return mm

        def pe_down(pe_, units, hT, half):
            for j in range(2):
                for i, n in enumerate(units):
                    mm = pe_.matmul(PS[i * PASS:(i + 1) * PASS, Y0 + half, :], hT[:, j, i * PASS:(i + 1) * PASS],
                                    slot(n + 2, 2)[:, j, half * 512:(half + 1) * 512],
                                    start=(j == 0), stop=(j == 1))
            return mm

        def pe_turn(pe_):
            for t in range(NT):
                pe_.transpose(PS[:, GU, 256 + t * P:256 + (t + 1) * P], hot_w[:, t, :], ident[:, :])
            for j in range(2):
                mm = pe_.transpose(PS[:, GU, j * P:(j + 1) * P], h_rows[:, j * P:(j + 1) * P], ident[:, :])
            return mm

        def pe_combine(pe_, rows, half):
            for t in range(NT):
                mm = pe_.matmul(OUT[t][:, half * 512:(half + 1) * 512], hot_wT[0:rows, t * P:(t + 1) * P],
                                y_rows[0:rows, half * 512:(half + 1) * 512], start=False, stop=False,
                                skip_group_check=True)
            return mm

        def table(eng, row, e):
            return eng.value_load(passes_i[0:1, row, bass.ds(e, 1)], min_val=0,
                                  max_val=MAX_PASSES - 1 if row == 0 else SEQ)

        def more_passes(eng, e, body):
            n = table(eng, 0, e)
            with eng.If(n > 0):
                first = table(eng, 1, e)
                with eng.Fori(0, n) as k:
                    body(first + k, k)

        def pe_moe(pe_, layer):
            m = moe_sem[layer]
            n_sh, n_ex = U_SHARED[layer], U_EXPERTS[layer]
            tag = f"ffn{layer}"
            pe_turn_rows(pe_, u, (rows_modulated, 2 * MODULATED.index(tag) + 2), tag)
            pe_.wait_ge(router_loaded, 16 * (layer + 1))
            for t in range(NT):
                for k in range(KC):
                    mm = pe_.matmul(PS[:, Y0, t * N_EXP:(t + 1) * N_EXP], uT[:, k, t * P:(t + 1) * P],
                                    w_router[:, k, :], start=(k == 0), stop=(k == KC - 1))
            mm.then_inc(m["router_out"], 1)
            for i in range(4):
                landed(pe_, n_sh + i // 2)
                for k in range(KC):
                    mm = pe_.matmul(PS[:, 4 + i // 2, (i % 2) * SEQ:(i % 2 + 1) * SEQ],
                                    slot(n_sh + i // 2)[:, k, (i % 2) * P:(i % 2 + 1) * P], uT[:, k, :],
                                    start=(k == 0), stop=(k == KC - 1))
                if i % 2:
                    mm.then_inc(unit_done, 1)
            pe_.wait_ge(m["mask_ready"], 1)
            R = PS[:, Y0 + 1, 0:NT * N_EXP].rearrange("p (t e) -> p t e", t=NT)
            pe_.matmul(R[:, 0, :], before[:, :], routed[:, 0, :], start=True, stop=True).then_inc(m["more_added"], 1)
            pe_.matmul(R[:, 1, :], ones[:, :], routed[:, 0, :], start=True, stop=False)
            pe_.matmul(R[:, 1, :], before[:, :], routed[:, 1, :], start=False, stop=True)
            lengths = PS[0:N_EXP, Y0 + 1, 256:256 + P]
            for t in range(NT):
                mm = pe_.matmul(lengths, routed[:, t, :], ones[:, :], start=(t == 0), stop=(t == NT - 1))
            mm.then_inc(m["ranks_out"], 1)
            pe_.wait_ge(m["shared_hid"], 1)
            landed(pe_, n_sh + 2)
            for t in range(NT):
                for half in range(2):
                    for j in range(2):
                        mm = pe_.matmul(OUT[t][:, half * 512:(half + 1) * 512], sh_hid[:, j, t * P:(t + 1) * P],
                                        slot(n_sh + 2, 2)[:, j, half * 512:(half + 1) * 512],
                                        start=(j == 0), stop=(j == 1))
            mm.then_inc(unit_done, 1)
            pe_.wait_ge(m["passes_ready"], 1)
            tables = PS[:, Y0, 128:128 + 2 * TABLE].rearrange("p (a e) -> p a e", a=2)
            pe_.matmul(tables[:, 0, 0:N_EXP], passes_f[0:N_EXP, :], ident[0:N_EXP, 0:N_EXP], start=True, stop=True)
            mm = pe_.matmul(tables[:, 1, :], passes_f[0:N_EXP, :], before[0:N_EXP, 0:TABLE], start=True, stop=True)
            mm.then_inc(m["passes_out"], 1)
            pe_.wait_ge(m["onehot_ready"], 4)
            pe_gather(pe_, one_hot[0], range(0, 4)).then_inc(m["gathered"], 1)
            pe_.wait_ge(m["x_ready"], 1)
            pe_gather(pe_, one_hot[0], range(4, 8)).then_inc(m["gathered"], 1)
            pe_.wait_ge(m["tables_ready"], 1)

            with pe_.Fori(0, TURNS) as turn:
                for q in range(BODY // 2):
                    pair = turn * 2 + q
                    units = (n_ex + 6 * q, n_ex + 6 * q + 3)
                    pe_.wait_ge(m["x_ready"], pair * 2 + 2)
                    for n in units:
                        for i in range(2):
                            pe_.wait_ge(slot_loaded[(n + i) % SLOTS], 16 * ((n + i) // SLOTS + 1) + turn * 16)
                    pe_gate_up(pe_, units, x_pair[q]).then_inc(m["gu_out"], 1)
                    pe_.wait_ge(m["onehot_ready"], pair * 4 + 8)
                    pe_gather(pe_, one_hot[1 - q], range(0, 4)).then_inc(m["gathered"], 1)
                    pe_.wait_ge(m["hot_w_ready"], pair * 4 + 4)
                    pe_.wait_ge(m["hid_ready"], pair + 1)
                    pe_turn(pe_).then_inc(m["turned"], 1)
                    pe_.wait_ge(m["x_ready"], pair * 2 + 3)
                    pe_gather(pe_, one_hot[1 - q], range(4, 8)).then_inc(m["gathered"], 1)
                    pe_.wait_ge(m["turned_copied"], pair + 1)
                    for n in units:
                        pe_.wait_ge(slot_loaded[(n + 2) % SLOTS], 16 * ((n + 2) // SLOTS + 1) + turn * 16)
                    for half in range(2):
                        pe_down(pe_, units, hidT, half).then_inc(m["y_out"], 1)
                    pe_.wait_ge(m["y_ready"], pair * 2 + 1)
                    pe_combine(pe_, 2 * PASS, 0)
                    pe_.wait_ge(m["y_ready"], pair * 2 + 2)
                    pe_combine(pe_, 2 * PASS, 1).then_inc(unit_done, 6)
                    pe_.wait_ge(m["x_ready"], pair * 2 + 4)
                    for x in range(2):
                        def one_more(i, k, n=units[x]):
                            pe_.wait_ge(m["more_onehot"], i * 4 + 4)
                            pe_gather(pe_, hot_more, range(KC)).then_inc(m["more_gathered"], 1)
                            pe_.wait_ge(m["more_x"], i + 1)
                            pe_gate_up(pe_, (n,), x_more).then_inc(m["more_gu"], 1)
                            pe_.wait_ge(m["more_hid"], i + 1)
                            pe_turn(pe_).then_inc(m["more_turned"], 1)
                            pe_.wait_ge(m["more_copied"], i + 1)
                            pe_down(pe_, (n,), hidT, 0)
                            pe_down(pe_, (n,), hidT, 1).then_inc(m["more_y_out"], 1)
                            pe_.wait_ge(m["more_y"], i * 2 + 2)
                            pe_combine(pe_, PASS, 0)
                            pe_combine(pe_, PASS, 1).then_inc(m["more_added"], 1)

                        more_passes(pe_, turn * BODY + (2 * q + x), one_more)

        def act_moe(done, layer):
            act, m = done.eng, moe_sem[layer]
            tag = f"ffn{layer}"
            act_row_norms(done, tag, (mix_added, 4 * layer + 4))
            act_copy_turned(done, uT, tag)
            act.wait_ge(m["router_out"], 1)
            done(act.activation(scores.rearrange("p t e -> p (t e)"), PS[:, Y0, 0:NT * N_EXP], ACT.Sigmoid),
                 m["scores_ready"])
            act.wait_ge(unit_done, U_SHARED[layer] + 1)
            done(act.activation(sh_act.rearrange("p j t -> p (j t)"), PS[:, 4, :], ACT.Silu), m["shared_act"])
            def copy_x(dst, half):
                return act.activation(dst[:, 4 * half:4 * half + 4, :].rearrange("p k s -> p (k s)"),
                                      PS[:, GATHER, :], ACT.Copy)

            for half in range(2):
                act.wait_ge(m["gathered"], half + 1)
                done(copy_x(x_pair[0], half), m["x_ready"])
            act.wait_ge(m["tables_ready"], 1)
            with act.Fori(0, TURNS) as turn:
                for q in range(BODY // 2):
                    pair = turn * 2 + q
                    act.wait_ge(m["gu_out"], pair + 1)
                    act.activation(gate_act, PS[:, GU, 0:D_EXP], ACT.Silu).then_inc(m["gate_ready"], 1)
                    act.wait_ge(m["gathered"], pair * 2 + 3)
                    copy_x(x_pair[1 - q], 0).then_inc(m["x_ready"], 1)
                    act.wait_ge(m["turned"], pair + 1)
                    act.activation(turned_sb, PS[:, GU, :], ACT.Copy).then_inc(m["turned_copied"], 1)
                    act.wait_ge(m["gathered"], pair * 2 + 4)
                    copy_x(x_pair[1 - q], 1).then_inc(m["x_ready"], 1)
                    for x in range(2):
                        def one_more(i, k):
                            act.wait_ge(m["more_gathered"], i + 1)
                            act.activation(x_more.rearrange("p k s -> p (k s)"), PS[:, GATHER, :],
                                           ACT.Copy).then_inc(m["more_x"], 1)
                            act.wait_ge(m["more_gu"], i + 1)
                            act.activation(gate_act[0:PASS], PS[0:PASS, GU, 0:D_EXP],
                                           ACT.Silu).then_inc(m["more_gate"], 1)
                            act.wait_ge(m["more_turned"], i + 1)
                            act.activation(turned_sb, PS[:, GU, :], ACT.Copy).then_inc(m["more_copied"], 1)

                        more_passes(act, turn * BODY + (2 * q + x), one_more)

        def dve_moe(done, layer, before_adding=None):
            dve, m = done.eng, moe_sem[layer]
            tag = f"ffn{layer}"
            dve_row_norms(done, tag)
            dve_modulate(done, ada[:, SH_F, :], ada[:, SC_F, :], [1, 4][layer], True, rows_modulated)
            done(dve.memset(slot_of[:, :, :], -1.0))
            done(dve.memset(weight_of[:, :, :], 0.0))
            done(dve.memset(passes_i[:, :, :], 0))
            dve.wait_ge(m["scores_ready"], 1)
            for t in range(NT):
                done(dve.tensor_tensor(chosen_by[:, t, :], scores[:, t, :], bias_router[:, layer, :], ALU.add))
                done(dve.max(top8[:, t, :], chosen_by[:, t, :]))
                done(dve.match_replace(replaced[:, t, :], top8[:, t, :], chosen_by[:, t, :], MASKED))
            done(dve.tensor_tensor(routed, replaced, chosen_by, ALU.not_equal), m["mask_ready"])
            done(dve.tensor_tensor(scores, scores, routed, ALU.mult))
            done(dve.tensor_reduce(rsum, scores, AX.X, ALU.add))
            done(dve.reciprocal(rsum, rsum))
            for t in range(NT):
                done(dve.tensor_scalar(weight_of[:, t, 0:N_EXP], scores[:, t, :], rsum[:, t:t + 1], ROUTED_SCALE,
                                       ALU.mult, ALU.mult))
            dve.wait_ge(m["ranks_out"], 1)
            R = PS[:, Y0 + 1, 0:NT * N_EXP].rearrange("p (t e) -> p t e", t=NT)
            done(dve.scalar_tensor_tensor(out=slot_of[:, :, 0:N_EXP], in0=R, scalar=1.0, in1=routed,
                                          op0=ALU.add, op1=ALU.mult))
            done(dve.tensor_scalar(slot_of[:, :, 0:N_EXP], slot_of[:, :, 0:N_EXP], -1.0, None, ALU.add))
            lengths = PS[0:N_EXP, Y0 + 1, 256:256 + P]
            pf = passes_f[0:N_EXP, :]
            done(dve.tensor_scalar(pf, lengths, float(PASS), None, ALU.is_gt))
            for i in range(2, MAX_PASSES):
                done(dve.scalar_tensor_tensor(out=pf, in0=lengths, scalar=float(i * PASS), in1=pf,
                                              op0=ALU.is_gt, op1=ALU.add),
                     m["passes_ready"] if i == MAX_PASSES - 1 else None)

            def hot(dst, t, e, first=0, at=0):
                return dve.tensor_scalar(dst[:, t, at:at + PASS], iota[:, bass.ds(first, PASS)], slot_of[:, t, bass.ds(e, 1)],
                                         None, ALU.is_equal)

            def hot_weighted(t, at, e, first=0):
                return dve.tensor_scalar(hot_w[:, t, at:at + PASS], iota[:, bass.ds(first, PASS)],
                                         slot_of[:, t, bass.ds(e, 1)], weight_of[:, t, bass.ds(e, 1)],
                                         ALU.is_equal, ALU.mult)

            for t in range(NT):
                for y in range(2):
                    done(hot(one_hot[0], t, y, at=y * PASS), m["onehot_ready"])
            dve.wait_ge(unit_done, U_SHARED[layer] + 2)
            dve.wait_ge(m["shared_act"], 1)
            done(dve.tensor_tensor(sh_hid.rearrange("p j t -> p (j t)"), sh_act.rearrange("p j t -> p (j t)"),
                                   PS[:, 5, :], ALU.mult), m["shared_hid"])
            for t in range(NT):
                for y in range(2):
                    done(hot(one_hot[1], t, 2 + y, at=y * PASS), m["onehot_ready"])
            dve.wait_ge(m["passes_out"], 1)
            tables = PS[0:1, Y0, 128:128 + 2 * TABLE].rearrange("p (a e) -> p a e", a=2)
            done(dve.tensor_copy(passes_i[:, 0, 0:N_EXP], tables[:, 0, 0:N_EXP]))
            done(dve.tensor_copy(passes_i[:, 1, :], tables[:, 1, :]), m["tables_ready"])

            with dve.Fori(0, TURNS) as turn:
                for q in range(BODY // 2):
                    pair = turn * 2 + q
                    e = turn * BODY + 2 * q
                    for y in range(2):
                        for t in range(NT):
                            hot_weighted(t, y * PASS, e + y).then_inc(m["hot_w_ready"], 1)
                    dve.wait_ge(m["gate_ready"], pair + 1)
                    dve.tensor_tensor(h_rows, gate_act, PS[:, GU, D_EXP:2 * D_EXP],
                                      ALU.mult).then_inc(m["hid_ready"], 1)
                    for y in range(2):
                        for t in range(NT):
                            hot(one_hot[q], t, e + 4 + y, at=y * PASS).then_inc(m["onehot_ready"], 1)
                    for half in range(2):
                        dve.wait_ge(m["y_out"], pair * 2 + half + 1)
                        dve.tensor_copy(y_rows[:, half * 512:(half + 1) * 512],
                                        PS[:, Y0 + half, :]).then_inc(m["y_ready"], 1)
                    for x in range(2):
                        e_ = turn * BODY + (2 * q + x)

                        def one_more(i, k, e_=e_):
                            for t in range(NT):
                                hot(hot_more, t, e_, (k + 1) * PASS).then_inc(m["more_onehot"], 1)
                                hot_weighted(t, 0, e_, (k + 1) * PASS).then_inc(m["more_onehot"], 1)
                            dve.wait_ge(m["more_gate"], i + 1)
                            dve.tensor_tensor(h_rows[0:PASS], gate_act[0:PASS],
                                              PS[0:PASS, GU, D_EXP:2 * D_EXP], ALU.mult).then_inc(m["more_hid"], 1)
                            dve.wait_ge(m["more_y_out"], i + 1)
                            for half in range(2):
                                dve.tensor_copy(y_rows[0:PASS, half * 512:(half + 1) * 512],
                                                PS[0:PASS, Y0 + half, :]).then_inc(m["more_y"], 1)

                        more_passes(dve, e_, one_more)
            if before_adding:
                before_adding()
            dve.wait_ge(unit_done, U_EXPERTS[layer] + 3 * N_EXP)
            dve.wait_ge(m["x_ready"], N_EXP + 2)
            total = table(dve, 1, N_EXP)
            dve.wait_ge(m["more_added"], total + 1)
            for t in range(NT):
                done(dve.tensor_tensor(g_tmp, OUT[t], ada[:, G_F, :], ALU.mult))
                done(dve.tensor_tensor(h[:, t, :], h[:, t, :], g_tmp, ALU.add),
                     layer_added)

        block = ctx.enter_context(nc.Block())

        @block.sync
        def _(sp):
            def load(n, src, k=KC, ready=None):
                if n >= SLOTS:
                    sp.wait_ge(unit_done, n - SLOTS + 1)
                sp.dma_start(slot(n, k), src).then_inc(slot_loaded[n % SLOTS], 16)

            def columns(n0, w, n):
                for j in range(n):
                    load(n0 + j, w[:, j * UC:(j + 1) * UC].rearrange("(k p) c -> p k c", p=P))

            def wide(w):
                return w.rearrange("(p k) c -> p k c", k=KC)

            def tall(w):
                return w.rearrange("(j p) c -> p j c", p=P)

            def experts(layer):
                n0 = U_EXPERTS[layer]
                m = moe_sem[layer]
                names = ("w_exp_gate", "w_exp_up", "w_exp_down")

                def fetch(r, src):
                    n = n0 + 3 * r
                    for i in range(3):
                        s = (n + i) % SLOTS
                        sp.dma_start(slot(n + i, 2 if i == 2 else KC), src(i)).then_inc(slot_loaded[s], 16)

                for r in range(BODY):
                    for i in range(3):
                        load(n0 + 3 * r + i, (tall if i == 2 else wide)(a[names[i]][layer, r]), 2 if i == 2 else KC)
                sp.wait_ge(m["tables_ready"], 1)
                with sp.Fori(1, TURNS) as turn:
                    for q in range(BODY // 2):
                        sp.wait_ge(unit_done, turn * SLOTS + (n0 + 6 * q - SLOTS + 6))
                        upto_pair = table(sp, 1, turn * BODY + (2 * q + 2 - BODY))
                        sp.wait_ge(m["more_added"], upto_pair + 1)
                        for x in range(2):
                            r = 2 * q + x

                            def src(i):
                                w = a[names[i]][layer, bass.ds(turn * BODY + r, 1), :, :]
                                if i == 2:
                                    return w.rearrange("o (j p) c -> p (o j) c", p=P)
                                return w.rearrange("o (p k) c -> p (o k) c", k=KC)

                            fetch(r, src)

            columns(U_ADA[0], a["w_ada"][0], 24)
            columns(U_QKV, a["w_in_a"][0], 12)
            columns(U_OUT_A, a["w_o_a"][0], 4)
            load(U_SHARED[0], wide(a["w_sh_gate"][0]))
            load(U_SHARED[0] + 1, wide(a["w_sh_up"][0]))
            load(U_SHARED[0] + 2, tall(a["w_sh_down"][0]), 2)
            experts(0)
            for q in range(BODY // 2):
                upto_pair = table(sp, 1, N_EXP - BODY + 2 * q + 2)
                sp.wait_ge(unit_done, U_ADA[1] - SLOTS + 6 * q + 6)
                sp.wait_ge(moe_sem[0]["more_added"], upto_pair + 1)
                for j in range(6 * q, 6 * q + 6):
                    load(U_ADA[1] + j, a["w_ada"][1][:, j * UC:(j + 1) * UC].rearrange("(k p) c -> p k c", p=P))
            for j in range(12, 24):
                load(U_ADA[1] + j, a["w_ada"][1][:, j * UC:(j + 1) * UC].rearrange("(k p) c -> p k c", p=P))
            columns(U_ADA_KV, a["w_ada_kv"], 8)
            columns(U_KV, a["w_kv_b"], 6)
            for c, name in enumerate(("w_cmp_k1", "w_cmp_v1")):
                for j in range(4):
                    load(U_CMP + 4 * c + j, a[name][j * D:(j + 1) * D, :].rearrange("(k p) c -> p k c", p=P))
            columns(U_Q, a["w_in_b"][0], 4)
            columns(U_OUT_B, a["w_o_b"][0], 4)
            load(U_SHARED[1], wide(a["w_sh_gate"][1]))
            load(U_SHARED[1] + 1, wide(a["w_sh_up"][1]))
            load(U_SHARED[1] + 2, tall(a["w_sh_down"][1]), 2)
            experts(1)
            for t in range(NT):
                sp.wait_ge(layer_added, NT + t + 1)
                sp.dma_start(out[0, t * P:(t + 1) * P, :], h[:, t, :]).then_inc(stored, 16)
            sp.wait_ge(stored, 16 * NT)

        @block.gpsimd
        def _(pool):
            def rows(name_ap):
                return name_ap.partition_broadcast(P)

            def first_row(rows_ap):
                return rows_ap[0:1].rearrange("p a d -> p (a d)")

            pool.dma_start(cond[:, :], a["c"].rearrange("o (k p) -> p (o k)", p=P),
                           allow_slow_non_contiguous=True).then_inc(cond_loaded, 16)
            pool.dma_start(first_row(ada[:, :, :]), a["b_ada"][0:1]).then_inc(bias_loaded, 16)
            done = Steps(pool, pool_step)
            done(pool.memset(ones[:, :], 1.0), ones_ready)
            pool.dma_start(pos_i[:, :], a["positions"].rearrange("o (t p) -> p (o t)", p=P),
                           allow_slow_non_contiguous=True).then_inc(params, 16)
            for t in range(NT):
                pool.dma_start(h[:, t, :], a["x"][0, t * P:(t + 1) * P, :]).then_inc(x_loaded, 16)
            pool.dma_start(gain[:, :], rows(a["norm_mix"][0])).then_inc(gain_loaded, 16)
            for dst, src in ((gain_qa, "qnorm_a"), (gain_ka, "knorm_a"), (gain_qb, "qnorm_b"),
                             (bias_f, "b_f_a"), (bias_gate, "b_gate_b")):
                pool.dma_start(dst[:, :], rows(a[src][0])).then_inc(params, 16)
            for i in range(3):
                pool.dma_start(gain_kb[:, i, :], rows(a["knorm_b"][i])).then_inc(params, 16)
            for i in range(2):
                pool.dma_start(bias_router[:, i, :], rows(a["b_router"][i])).then_inc(params, 16)
            for i, name in enumerate(("pe_cmp_k", "pe_cmp_v")):
                for half in range(2):
                    pool.dma_start(pe[half * CMP:(half + 1) * CMP, i, :], a[name]).then_inc(params, 16)
            pool.dma_start(w_forget, a["w_in_a"][0][:, 3 * D:3 * D + H].rearrange("(k p) c -> p k c", p=P)
                           ).then_inc(params, 16)
            done(pool.memset(ident[:, :], 0.0))
            done(pool.memset(causal[:, :], 0.0))
            done(pool.memset(upto[:, :], 1.0))
            done(pool.memset(before[:, :], 1.0))
            done(pool.memset(block_diag[:, :], 1.0))
            done(pool.affine_select(out=ident[:, :], in_=ident[:, :], compare_op=ALU.not_equal, fill=1.0,
                                    base=0, pattern=[[-1, P]], channel_multiplier=1))
            done(pool.affine_select(out=upto[:, :], in_=upto[:, :], compare_op=ALU.is_ge, fill=0.0,
                                    base=0, pattern=[[1, P]], channel_multiplier=-1))
            done(pool.affine_select(out=before[:, :], in_=before[:, :], compare_op=ALU.is_ge, fill=0.0,
                                    base=-1, pattern=[[1, P]], channel_multiplier=-1))
            done(pool.affine_select(out=causal[:, P:2 * P], in_=causal[:, P:2 * P], compare_op=ALU.is_ge,
                                    fill=MASKED, base=0, pattern=[[-1, P]], channel_multiplier=1))
            done(pool.affine_select(out=block_diag[:, :], in_=block_diag[:, :], compare_op=ALU.is_ge, fill=0.0,
                                    base=0, pattern=[[-NB, H]], channel_multiplier=1))
            done(pool.affine_select(out=block_diag[:, :], in_=block_diag[:, :], compare_op=ALU.is_ge, fill=0.0,
                                    base=NB - 1, pattern=[[NB, H]], channel_multiplier=-1))
            for i in range(ROPE_HALF):
                f = np.float32(ROPE_THETA) ** np.float32(-2 * i / (2 * ROPE_HALF))
                done(pool.memset(freq[:, i:i + 1], float(f)))
            done(pool.iota(partition_no[:, :], pattern=[[0, 1]], base=0, channel_multiplier=1,
                           allow_small_or_imprecise_dtypes=True))
            done(pool.iota(iota[:, :], pattern=[[1, SEQ]], base=0, channel_multiplier=0,
                           allow_small_or_imprecise_dtypes=True), consts)
            for i, src in enumerate((a["norm_ffn"][0], a["norm_kv"], a["norm_mix"][1], a["norm_ffn"][1])):
                pool.wait_ge(gain_used, i + 1)
                pool.dma_start(gain[:, :], rows(src)).then_inc(gain_loaded, 16)
                if i in (0, 3):
                    layer = i // 3
                    pool.wait_ge(mix_added, 4 * layer + 4)
                    pool.dma_start(w_router, a["w_router"][layer].rearrange("(p k) c -> p k c", k=KC)
                                   ).then_inc(router_loaded, 16)
                if i == 0:
                    pool.dma_start(w_gates[:, :, :], a["w_in_b"][0][:, D:D + 3 * H].rearrange(
                        "(k p) c -> p k c", p=P)).then_inc(nsa_params, 16)
                    pool.wait_ge(moe_sem[0]["tables_ready"], 1)
                    pool.dma_start(first_row(ada[:, 0:G_F, :]), a["b_ada"][1:2, 0:G_F * D]).then_inc(bias_loaded, 16)
                    pool.wait_ge(layer_added, NT)
                    pool.dma_start(first_row(ada[:, G_F:, :]), a["b_ada"][1:2, G_F * D:]
                                   ).then_inc(late_biases_loaded, 16)
                    for c, name in enumerate(("w_cmp_k2", "w_cmp_v2")):
                        pool.dma_start(w_cmp2[:, c, :, :], a[name].rearrange("(j p) c -> p j c", p=P)
                                       ).then_inc(nsa_params, 16)
                    pool.dma_start(first_row(ada_kv), a["b_ada_kv"].rearrange("(o c) -> o c", o=1)
                                   ).then_inc(late_biases_loaded, 16)

        N_PARAMS = 1 + 5 + 3 + 2 + 4 + 1
        fox_batches = attention_batches("fox")
        nsa_batches = attention_batches("nsa")

        @block.tensor
        def _(pe_):
            pe_.wait_ge(cond_ready, 2)
            pe_.wait_ge(ones_ready, 1)
            pe_ada(pe_, 0)
            pe_.wait_ge(consts, 1)

            pe_turn_rows(pe_, u, (rows_modulated, 2 * MODULATED.index("mix0") + 2), "mix0")

            def turn_unit(j):
                pe_.wait_ge(sem("fox_normed"), j + 1)
                if j >= 2:
                    pe_.wait_ge(sem("fox_copied"), j - 1 if j - 2 < 4 else 4 + 2 * (j - 2 - 3))
                src = normed[j % 2].rearrange("p (t c) -> p t c", t=NT)
                for c in range(2):
                    for t in range(NT):
                        mm = pe_.transpose(PS[:, 4 + j % 2, c * SEQ + t * P:c * SEQ + (t + 1) * P],
                                           src[:, t, c * P:(c + 1) * P], ident[:, :])
                mm.then_inc(sem("fox_turned"), 1)

            for j in range(12):
                if j >= 4:
                    if j - 4 < 8:
                        pe_.wait_ge(sem("fox_normed"), j - 3)
                pe_rows_unit(pe_, U_QKV + j, j % 4, uT)
                if 1 <= j <= 8:
                    turn_unit(j - 1)
            pe_.wait_ge(params, 16 * N_PARAMS)
            for t in range(NT):
                for k in range(KC):
                    mm = pe_.matmul(PS[:, 6, t * H:(t + 1) * H], uT[:, k, t * P:(t + 1) * P], w_forget[:, k, :],
                                    start=(k == 0), stop=(k == KC - 1))
            mm.then_inc(sem("forget_out"), 1)
            lf = fg[4].rearrange("p (t h) -> p t h", t=NT)
            pe_.wait_ge(sem("logf_ready"), 1)
            pe_.matmul(PS[:, 7, 0:H], upto[:, :], lf[:, 0, :], start=True, stop=True)
            pe_.matmul(PS[:, 7, H:2 * H], ones[:, :], lf[:, 0, :], start=True, stop=False)
            pe_.matmul(PS[:, 7, H:2 * H], upto[:, :], lf[:, 1, :], start=False, stop=True).then_inc(sem("cum_out"), 1)
            pe_.wait_ge(sem("cum_ready"), 1)
            for t in range(NT):
                mm = pe_.transpose(PS[:, 6, t * P:(t + 1) * P], cum[:, t, :], ident[:, :])
            mm.then_inc(sem("cum_turned"), 1)
            pe_.wait_ge(sem("cumT_ready"), 1)
            pe_.wait_ge(sem("fox_copied"), 12)
            pe_.wait_ge(sem("fox_v"), 4)
            pe_attention(pe_, "fox", fox_batches, lambda br, hd: kz_a[:, hd, :],
                         lambda br, kt, hd: v_a[:, kt, hd * DH:(hd + 1) * DH])
            pe_turn_rows(pe_, u, (heads_read, 8), "fox_o")
            for j in range(4):
                pe_rows_unit(pe_, U_OUT_A + j, 4 + j, uT)
            pe_.wait_ge(mix_added, 4)
            pe_moe(pe_, 0)

            pe_.wait_ge(cond_ready, 3)
            pe_ada(pe_, 1)
            pe_turn_rows(pe_, u, (rows_modulated, 2 * MODULATED.index("kv") + 2), "kv")
            for j in range(6):
                if j >= 4:
                    pe_.wait_ge(sem("kv_doubled"), j - 3)
                pe_rows_unit(pe_, U_KV + j, j % 4, uT)
            for i in range(4):
                pe_.wait_ge(sem("kv_doubled"), i + 1)
                if i >= 1:
                    pe_.wait_ge(sem("kv_copied"), [0, 8, 16, 18][i])
                for g in range(G):
                    for t in range(NT):
                        mm = pe_.transpose(PS[:, 4 + g // 2, (g % 2) * SEQ + t * P:(g % 2) * SEQ + (t + 1) * P],
                                           doubled[i % 2][:, t, g].rearrange("p a d -> p (a d)"), ident[:, :])
                mm.then_inc(sem("kv_turned2"), 1)
            pe_.wait_ge(sem("kv_copied"), 20)
            pe_.wait_ge(nsa_params, 16 * 3)
            for c in range(2):
                if c == 1:
                    pe_.wait_ge(sem("cmp_hidden"), 2)
                for j in range(4):
                    n = U_CMP + 4 * c + j
                    landed(pe_, n)
                    for k in range(KC):
                        for i in range(2):
                            mm = pe_.matmul(PS[:, 4 + i, 0:G * NB], slot(n)[:, k, i * P:(i + 1) * P],
                                            flat[c][:, KC * j + k, :], start=(j + k == 0), stop=(j == 3 and k == 7))
                    mm.then_inc(unit_done, 1)
                if c == 0:
                    pe_.wait_ge(sem("cmp_hidden"), 2)
                    for i in range(2):
                        mm = pe_.matmul(PS[0:G * NB, 6, 0:DH], hidden[:, i, :], w_cmp2[:, 0, i, :],
                                        start=(i == 0), stop=(i == 1))
                    mm.then_inc(sem("cmp_k"), 1)
                    pe_.wait_ge(sem("cmp_k_normed"), 1)
                    pe_.transpose(PS[:, 6, 0:G * NB], kc_rows[0:G * NB].rearrange("p a d -> p (a d)"),
                                  ident[0:G * NB, 0:G * NB]).then_inc(sem("cmp_k_turned"), 1)
                else:
                    pe_.wait_ge(sem("cmp_rep"), 2)
                    for i in range(2):
                        mm = pe_.matmul(PS[0:H * NB, 7, 0:DH], hidden_rep[:, i, :], w_cmp2[:, 1, i, :],
                                        start=(i == 0), stop=(i == 1))
                    mm.then_inc(sem("cmp_v"), 1)
            pe_turn_rows(pe_, u, (rows_modulated, 2 * MODULATED.index("mix1") + 2), "mix1",
                         [(sem("kv_doubled"), 4), (sem("kv_values"), 2), (sem("kcz_ready"), 2)])
            for t in range(NT):
                for k in range(KC):
                    mm = pe_.matmul(PS[:, 6, t * 3 * H:(t + 1) * 3 * H], uT[:, k, t * P:(t + 1) * P],
                                    w_gates[:, k, :], start=(k == 0), stop=(k == KC - 1))
            mm.then_inc(sem("gates_out"), 1)
            for j in range(4):
                pe_rows_unit(pe_, U_Q + j, j, uT)
            pe_turn_rows(pe_, q_rows, (sem("q_normed"), 4), "q")
            pe_.wait_ge(sem("gates_ready"), 1)
            for t in range(NT):
                for hd in range(H):
                    g = hd // HPG
                    mm = pe_.matmul(PS[:, 6, t * H * NB + hd * NB:t * H * NB + (hd + 1) * NB],
                                    qT[:, hd // 2, t * P:(t + 1) * P], kcz[:, hd % 2, g * NB:(g + 1) * NB],
                                    start=True, stop=True)
            mm.then_inc(sem("cmp_logits"), 1)
            pe_.wait_ge(sem("cmp_probs"), NT)
            for t in range(NT):
                mm = pe_.transpose(PS[0:H * NB, 7, t * P:(t + 1) * P], cmp_buf[:, t, :], ident[:, :])
            mm.then_inc(sem("cmp_probs_turned"), 1)
            pe_.wait_ge(sem("cmp_probsT"), 1)
            for t in range(NT):
                for half in range(2):
                    pe_.matmul(PS[:, 2 * t + half, :], cmp_T[0:H * NB, t * P:(t + 1) * P],
                               v_diag[0:H * NB, 8 * half:8 * half + 8, :].rearrange("p h d -> p (h d)"),
                               start=True, stop=True).then_inc(sem("cmp_heads"), 1)
            pe_.wait_ge(sem("cmp_heads_read"), 2)
            pe_turn_rows(pe_, q_rows, (sem("q_rotated"), 1), "q_rotated")
            pe_attention(pe_, "nsa", nsa_batches, lambda br, hd: kz_b[:, br, hd // HPG, hd % 2, :],
                         lambda br, kt, hd: v_b[:, br, kt, (hd // HPG) * DH:(hd // HPG + 1) * DH])
            pe_turn_rows(pe_, u, (sem("nsa_o"), 16), "nsa_o")
            for j in range(4):
                pe_rows_unit(pe_, U_OUT_B + j, 4 + j, uT)
            pe_.wait_ge(mix_added, 8)
            pe_moe(pe_, 1)

        @block.scalar
        def _(act):
            done = Steps(act, act_step)
            act.wait_ge(cond_loaded, 16)
            done(act.activation(cond[:, :], cond[:, :], ACT.Silu), cond_ready)
            act_ada(done, 0, 0, ADA_FIRST)
            act.wait_ge(sem("angles"), 2)
            done(act.activation(sin_t[:, :, :], sin_t[:, :, :], ACT.Sin))
            done(act.activation(cos_t[:, :, :], cos_t[:, :, :], ACT.Sin), sem("rope_ready"))
            act_row_norms(done, "mix0", (x_loaded, 16 * NT))
            act_ada(done, 0, ADA_FIRST, 24)
            act_copy_turned(done, uT, "mix0")
            copied = sem("fox_copied")

            def copy_unit(j):
                act.wait_ge(sem("fox_turned"), j + 1)
                src = PS[:, 4 + j % 2, :].rearrange("p (c t) -> p c t", c=2)
                if j < 4:
                    done(act.activation(qT[:, 2 * j:2 * j + 2, :], src, ACT.Copy), copied)
                else:
                    hd = 4 * (j - 4)
                    for par in range(2):
                        rows = slice(par * DH, (par + 1) * DH)
                        done(act.activation(kz_a[rows, hd + par:hd + 4:2, :], src[rows], ACT.Copy), copied)

            act.wait_ge(sem("kz_zeroed"), 1)
            for j in range(8):
                act_head_squares(done, "foxn", j, U_QKV + j, j % 4)
                if j >= 1:
                    copy_unit(j - 1)
            copy_unit(7)
            for j in range(4):
                act.wait_ge(unit_done, U_QKV + 8 + j + 1)
                done(act.activation(v_a[:, :, j * UC:(j + 1) * UC],
                                    PS[:, j % 4, :].rearrange("p (t c) -> p t c", t=NT), ACT.Copy), sem("fox_v"))
            act.wait_ge(sem("forget_abs"), 1)
            done(act.activation(fg[2], fg[1], ACT.Exp, scale=-1.0), sem("forget_exp"))
            act.wait_ge(sem("forget_1p"), 1)
            done(act.activation(fg[3], fg[2], ACT.Ln), sem("forget_ln"))
            act_attention(done, "fox", fox_batches)
            act_copy_turned(done, uT, "fox_o")
            act_moe(done, 0)
            act_ada(done, 1, 0, ADA_ALONE[1])
            act_row_norms(done, "mix1", (layer_added, NT))
            act_ada(done, 1, ADA_ALONE[1], 32)
            act_copy_turned(done, uT, "kv")
            def key_norm_and_values(i):
                c = 2 + 2 * i
                act_head_squares(done, "kvn", i, U_KV + c, c % 4, squares_kv)
                act.wait_ge(unit_done, U_KV + c + 2)
                done(act.activation(v_b[:, i], PS[:, (c + 1) % 4, :].rearrange("p (t c) -> p t c", t=NT), ACT.Copy),
                     sem("kv_values"))

            for i in range(4):
                if i in (0, 2):
                    key_norm_and_values(i // 2)
                act.wait_ge(sem("kv_turned2"), i + 1)
                src = PS[:, 4:6, :].rearrange("p b (g t) -> p (b g) t", g=2)
                for par in range(2):
                    rows = slice(par * DH, (par + 1) * DH)
                    if i < 2:
                        for g in range(G):
                            v = src[rows, g].rearrange("p (n m a) -> p a n m", n=NB, a=2)[:, par]
                            o = flat[i][rows, :, g * NB:(g + 1) * NB].rearrange("p m n -> p n m")
                            done(act.activation(o, v, ACT.Copy), sem("kv_copied"))
                    else:
                        done(act.activation(kz_b[rows, i - 2, :, par, :], src[rows], ACT.Copy), sem("kv_copied"))
            for c in range(2):
                act.wait_ge(unit_done, U_CMP + 4 * c + 4)
                if c == 1:
                    act.wait_ge(sem("cmp_k"), 1)
                for i in range(2):
                    done(act.activation(hidden[:, i, :], PS[:, 4 + i, 0:G * NB], ACT.Silu), sem("cmp_hidden"))
                if c == 0:
                    act.wait_ge(sem("cmp_k"), 1)
                    done(act.activation(kc_rows[0:G * NB, 0, :], PS[0:G * NB, 6, 0:DH], ACT.Square,
                                        accum_out=small[0:G * NB, 72:73]), sem("cmp_k_sq"))
                    act.wait_ge(sem("cmp_k_mean"), 1)
                    done(act.activation(small[0:G * NB, 74:75], small[0:G * NB, 73:74], ACT.Sqrt), sem("cmp_k_root"))
            act_copy_turned(done, uT, "mix1")
            act.wait_ge(sem("gates_biased"), 1)
            done(act.activation(gates[:, :, :], gates[:, :, :], ACT.Sigmoid), sem("gates_ready"))
            for j in range(4):
                act_head_squares(done, "qn", j, U_Q + j, j)
            act_copy_turned(done, qT, "q")
            act.wait_ge(sem("cmp_shifted"), NT)
            done(act.activation(cmp_buf, cmp_buf, ACT.Exp), sem("cmp_exp"))
            act.wait_ge(sem("cmp_probs_turned"), 1)
            done(act.activation(cmp_T[0:H * NB, :], PS[0:H * NB, 7, 0:SEQ], ACT.Copy), sem("cmp_probsT"))
            act_copy_turned(done, qT, "q_rotated")
            act_attention(done, "nsa", nsa_batches)
            act_copy_turned(done, uT, "nsa_o")
            act_moe(done, 1)

        @block.vector
        def _(dve):
            done = Steps(dve, dve_step)
            def signal_cond():
                dve.tensor_copy(cond_cols, cond[:, :].unsqueeze(2).to_broadcast([P, KC, P])).then_inc(cond_ready, 1)

            dve.wait_ge(cond_ready, 1)
            signal_cond()
            dve.wait_ge(cond_ready, 2)
            dve_ada(done, 0, 0, ADA_FIRST)
            dve.wait_ge(consts, 1)
            dve.wait_ge(params, 16 * N_PARAMS)
            TWO_PI = 2 * np.pi
            c1 = 6.28125
            c2 = float(np.float32(np.float16(TWO_PI - c1)))
            c3 = float(TWO_PI - c1 - c2)
            BIG = 1.5 * 2.0 ** 23
            pos_f, turns, tmp = small[:, 0:2], small[:, 2:18], small[:, 18:34]
            ang = sin_t[:, :, :].rearrange("p t r -> p (t r)")
            cosv = cos_t[:, :, :].rearrange("p t r -> p (t r)")
            done(dve.tensor_copy(pos_f, pos_i[:, :]))
            for t in range(NT):
                done(dve.tensor_scalar(sin_t[:, t, :], freq[:, :], pos_f[:, t:t + 1], None, ALU.mult))
            done(dve.tensor_scalar(turns, ang, 1.0 / TWO_PI, None, ALU.mult))
            done(dve.tensor_scalar(turns, turns, BIG, None, ALU.add))
            done(dve.tensor_scalar(turns, turns, -BIG, None, ALU.add))
            for c in (c1, c2, c3):
                done(dve.scalar_tensor_tensor(out=ang, in0=turns, scalar=-c, in1=ang, op0=ALU.mult, op1=ALU.add))

            def fold(x, last=None):
                done(dve.tensor_scalar(tmp, x, float(np.pi), -TWO_PI, ALU.is_gt, ALU.mult))
                done(dve.tensor_tensor(x, x, tmp, ALU.add))
                done(dve.tensor_scalar(x, x, 3.1415925, -3.1415925, ALU.min, ALU.max), last)

            done(dve.tensor_scalar(cosv, ang, float(np.pi / 2), None, ALU.add))
            fold(cosv, sem("angles"))
            fold(ang, sem("angles"))
            done(dve.tensor_scalar(gain_qa[:, :], gain_qa[:, :], QK_SCALE, None, ALU.mult))
            done(dve.tensor_scalar(gain_qb[:, :], gain_qb[:, :], QK_SCALE, None, ALU.mult))
            dve.wait_ge(x_loaded, 16 * NT)
            dve_row_norms(done, "mix0")
            done(dve.memset(kz_a, 0.0), sem("kz_zeroed"))
            dve_ada(done, 0, ADA_FIRST, 24)
            dve.wait_ge(ada_read, 24)
            dve_modulate(done, ada[:, SH_M, :], ada[:, SC_M, :], 0, False, rows_modulated)
            done(dve.tensor_copy(head_row, ident[:, 0:H].unsqueeze(2).to_broadcast([P, H, P])))
            for j in range(8):
                if j >= 2:
                    dve.wait_ge(sem("fox_turned"), j - 1)
                dve_head_norm(done, "foxn", j, j % 4,
                              normed[j % 2].rearrange("p (t h d) -> p t h d", t=NT, h=4),
                              (gain_qa if j < 4 else gain_ka)[:, :], sem("fox_normed"))
            dve.wait_ge(sem("forget_out"), 1)
            z, az, ez, lnz, logf = fg
            done(dve.tensor_tensor(z.rearrange("p (t h) -> p t h", t=NT),
                                   PS[:, 6, 0:2 * H].rearrange("p (t h) -> p t h", t=NT),
                                   bias_f[:, :].unsqueeze(1).to_broadcast([P, NT, H]), ALU.add))
            done(dve.tensor_scalar(az, z, -1.0, None, ALU.mult))
            done(dve.tensor_tensor(az, az, z, ALU.max), sem("forget_abs"))
            done(dve.memset(cum, 0.0))
            dve.wait_ge(sem("forget_exp"), 1)
            done(dve.tensor_scalar(ez, ez, 1.0, None, ALU.add), sem("forget_1p"))
            done(dve.tensor_scalar(z, z, 0.0, None, ALU.min))
            dve.wait_ge(sem("forget_ln"), 1)
            done(dve.tensor_tensor(logf, z, lnz, ALU.subtract), sem("logf_ready"))
            dve.wait_ge(sem("cum_out"), 1)
            done(dve.tensor_copy(cum[:, :, 0:H], PS[:, 7, 0:2 * H].rearrange("p (t h) -> p t h", t=NT)),
                 sem("cum_ready"))
            dve.wait_ge(sem("cum_turned"), 1)
            done(dve.tensor_copy(cumT, PS[:, 6, 0:SEQ]))
            done(dve.tensor_scalar(ncumT, cumT, -1.0, None, ALU.mult), sem("cumT_ready"))

            def fox_finish(b, heads, rinv):
                br, t, g = fox_batches[b]
                dve.wait_ge(heads_out, b + 1)
                done(dve.tensor_tensor(u[:, t, g * UC:(g + 1) * UC].rearrange("p (i d) -> p i d", i=4), heads,
                                       rinv.unsqueeze(2).to_broadcast([P, 4, DH]), ALU.mult), heads_read)

            dve_attention(done, "fox", fox_batches, fox_finish)

            def add_mix(layer, u0):
                for j in range(4):
                    dve.wait_ge(unit_done, u0 + j + 1)
                    cols = slice(j * UC, (j + 1) * UC)
                    dve_add_rows(done, cols, PS[:, 4 + j, :].rearrange("p (t c) -> p t c", t=NT),
                                 ada[:, G_M, cols], mix_added)

            add_mix(0, U_OUT_A)
            dve_moe(done, 0, signal_cond)

            dve_row_norms(done, "mix1")
            dve_ada(done, 1, 0, 32)
            dve.wait_ge(ada_read, ada_read_before(1) + 32)
            dve_modulate(done, ada_kv[:, 0, :], ada_kv[:, 1, :], 2, False, rows_modulated)
            done(dve.memset(kz_b, 0.0))
            done(dve.memset(small[:, 0:32], 0.0))
            for j in range(2):
                dve.wait_ge(unit_done, U_KV + j + 1)
                for t in range(NT):
                    for c in range(2):
                        done(dve.tensor_tensor(doubled[j][:, t, :, c, :],
                                               PS[:, j, t * UC:(t + 1) * UC].rearrange("p (g d) -> p g d", g=G),
                                               pe[:, j, :].unsqueeze(1).to_broadcast([P, G, DH]), ALU.add),
                             sem("kv_doubled") if t == 1 and c == 1 else None)
            for i, j in enumerate((2, 4)):
                dve.wait_ge(sem("kv_turned2"), i + 1)
                dve_head_norm(done, "kvn", i, j % 4, new_keys, gain_kb[:, 1 + i, :], None, squares_kv)
                dve_rope(done, new_keys, G, rope_tmp_k, None)
                for t in range(NT):
                    for c in range(2):
                        done(dve.tensor_copy(doubled[i][:, t, :, c, :], new_keys[:, t]),
                             sem("kv_doubled") if (t == 1 and c == 1) else None)
            dve.wait_ge(sem("cmp_k_sq"), 1)
            R16 = slice(0, G * NB)
            done(dve.tensor_scalar(small[R16, 73:74], small[R16, 72:73], 1.0 / DH, EPS, ALU.mult, ALU.add),
                 sem("cmp_k_mean"))
            dve.wait_ge(sem("cmp_k_root"), 1)
            done(dve.reciprocal(small[R16, 75:76], small[R16, 74:75]))
            for c in range(2):
                done(dve.scalar_tensor_tensor(out=kc_rows[R16, c, :], in0=PS[R16, 6, 0:DH],
                                              scalar=small[R16, 75:76], in1=gain_kb[R16, 0, :],
                                              op0=ALU.mult, op1=ALU.mult), sem("cmp_k_normed") if c else None)
            dve.wait_ge(sem("cmp_k_turned"), 1)
            for par in range(2):
                rows = slice(par * DH, (par + 1) * DH)
                done(dve.tensor_copy(kcz[rows, par, :], PS[rows, 6, 0:G * NB]), sem("kcz_ready"))
            dve.wait_ge(sem("cmp_hidden"), 4)
            for i in range(2):
                done(dve.tensor_copy(hidden_rep[:, i, :].rearrange("p (g i n) -> p g i n", g=G, i=HPG),
                                     hidden[:, i, :].rearrange("p (g n) -> p g n", g=G).unsqueeze(2)
                                     .to_broadcast([P, G, HPG, NB])), sem("cmp_rep"))
            dve.wait_ge(sem("cmp_v"), 1)
            RV = slice(0, H * NB)
            done(dve.tensor_copy(v_cmp_rows[RV, :], PS[RV, 7, 0:DH]))
            done(dve.tensor_tensor(v_diag[RV], v_cmp_rows[RV, :].unsqueeze(1).to_broadcast([H * NB, H, DH]),
                                   block_diag[:, :].unsqueeze(2).to_broadcast([H * NB, H, DH]), ALU.mult))
            dve_modulate(done, ada[:, SH_M, :], ada[:, SC_M, :], 3, False, rows_modulated, mod_tmp_q)
            dve.wait_ge(sem("gates_out"), 1)
            done(dve.tensor_tensor(gates[:, :, :], PS[:, 6, 0:NT * 3 * H].rearrange("p (t c) -> p t c", t=NT),
                                   bias_gate[:, :].unsqueeze(1).to_broadcast([P, NT, 3 * H]), ALU.add),
                 sem("gates_biased"))
            for j in range(4):
                dve_head_norm(done, "qn", j, j,
                              q_rows[:, :, j * UC:(j + 1) * UC].rearrange("p t (h d) -> p t h d", h=4),
                              gain_qb[:, :], sem("q_normed"))
            for t in range(NT):
                for n in range(NB):
                    first = (n + 1) * CMP - 1 - t * P
                    if first <= 0:
                        done(dve.memset(visible[:, t, n:n + 1], 1.0))
                    elif first >= P:
                        done(dve.memset(visible[:, t, n:n + 1], 0.0))
                    else:
                        done(dve.tensor_scalar(visible[:, t, n:n + 1], partition_no[:, :], float(first),
                                               None, ALU.is_ge))
            done(dve.tensor_scalar(hidden_mask, visible, -1.0, -MASKED, ALU.add, ALU.mult))
            dve.wait_ge(sem("cmp_logits"), 1)
            for t in range(NT):
                x = cmp_buf[:, t, :].rearrange("p (h n) -> p h n", h=H)
                src = PS[:, 6, t * H * NB:(t + 1) * H * NB].rearrange("p (h n) -> p h n", h=H)
                done(dve.tensor_tensor(x, src, visible[:, t, :].unsqueeze(1).to_broadcast([P, H, NB]), ALU.mult))
                done(dve.tensor_tensor(x, x, hidden_mask[:, t, :].unsqueeze(1).to_broadcast([P, H, NB]), ALU.add))
                done(dve.tensor_reduce(small[:, 32:48], x, AX.X, ALU.max))
                done(dve.tensor_tensor(x, x, small[:, 32:48].unsqueeze(2).to_broadcast([P, H, NB]), ALU.subtract),
                     sem("cmp_shifted"))
            dve.wait_ge(sem("cmp_exp"), 1)
            for t in range(NT):
                x = cmp_buf[:, t, :].rearrange("p (h n) -> p h n", h=H)
                done(dve.tensor_reduce(small[:, 32:48], x, AX.X, ALU.add))
                done(dve.reciprocal(small[:, 32:48], small[:, 32:48]))
                done(dve.tensor_tensor(x, x, visible[:, t, :].unsqueeze(1).to_broadcast([P, H, NB]), ALU.mult))
                done(dve.tensor_tensor(x, x, small[:, 32:48].unsqueeze(2).to_broadcast([P, H, NB]), ALU.mult),
                     sem("cmp_probs"))

            def gate_of(t, h0, n, br):
                return gates[:, t, :].rearrange("p (h b) -> p b h", b=3)[:, br, h0:h0 + n]

            dve.wait_ge(rows_turned, 4 * TURNED.index("q") + 4)
            dve_rope(done, q_rows.rearrange("p t (h d) -> p t h d", h=H), H, rope_tmp_q, sem("q_rotated"))
            for t in range(NT):
                dve.wait_ge(sem("cmp_heads"), 2 * t + 2)
                done(dve.tensor_tensor(u[:, t, :].rearrange("p (h d) -> p h d", h=H),
                                       PS[:, 2 * t:2 * t + 2, :].rearrange("p b (h d) -> p (b h) d", h=8),
                                       gate_of(t, 0, H, 0).unsqueeze(2).to_broadcast([P, H, DH]), ALU.mult),
                     sem("cmp_heads_read"))

            def nsa_finish(b, heads, rinv):
                br, t, g = nsa_batches[b]
                dve.wait_ge(heads_out, BATCHES_FROM["nsa"] + b + 1)
                done(dve.tensor_tensor(rinv, rinv, gate_of(t, 4 * g, 4, 1 + br), ALU.mult))
                done(dve.tensor_tensor(head_tmp, heads, rinv.unsqueeze(2).to_broadcast([P, 4, DH]), ALU.mult),
                     heads_read)
                o = u[:, t, g * UC:(g + 1) * UC].rearrange("p (i d) -> p i d", i=4)
                done(dve.tensor_tensor(o, o, head_tmp, ALU.add), sem("nsa_o"))

            dve_attention(done, "nsa", nsa_batches, nsa_finish)
            add_mix(1, U_OUT_B)
            dve_moe(done, 1)


_INS = ["x", "c", "positions", "w_ada", "b_ada", "norm_mix", "norm_ffn", "w_in_a", "b_f_a", "qnorm_a", "knorm_a",
        "w_o_a", "norm_kv", "w_ada_kv", "b_ada_kv", "w_kv_b", "pe_cmp_k", "pe_cmp_v", "w_cmp_k1", "w_cmp_k2",
        "w_cmp_v1", "w_cmp_v2", "knorm_b", "w_in_b", "b_gate_b", "qnorm_b", "w_o_b", "w_router", "b_router",
        "w_exp_gate", "w_exp_up", "w_exp_down", "w_sh_gate", "w_sh_up", "w_sh_down"]


def kernel(**inputs):
    import numpy as _np
    import concourse.bacc as _bacc
    from concourse import mybir as _mybir
    from concourse.bass_utils import run_bass_kernel_spmd as _run

    nc = _bacc.Bacc("TRN2", target_bir_lowering=False, num_devices=1)
    arrays, args = {}, {}
    for name in _INS:
        x = _np.ascontiguousarray(inputs[name])
        arrays[f"in_{name}"] = x
        args[name] = nc.dram_tensor(f"in_{name}", x.shape, _mybir.dt.from_np(x.dtype), kind="ExternalInput").ap()
    out = nc.dram_tensor("out_0", (1, SEQ, D), _mybir.dt.float32, kind="ExternalOutput").ap()
    build(nc, args, out)
    r = _run(nc, [arrays], core_ids=[0])
    return r.results[0]["out_0"]
```
